# Optimizing a Trainium2 kernel written in Bass

```python
import math
import jax, jax.numpy as jnp
from jax import lax
import numpy as np

D_MODEL = 1024
BATCH = 1
SEQ = 1024
DEPTH = 2
DEC_BATCH = 1
DEC_SEQ = 1024
PAST_LEN = 128

N_MIXERS = 2
HEAD_DIM = 64
N_HEADS_A = 16
DILATIONS = ((128, 1), (512, 4), (2048, 16))
N_DIL = len(DILATIONS)
DIL_BLOCK_Q = 64
N_BUCKETS = 32
T5_MAX_DISTANCE = 1024
N_HEADS_B = 16
GRID_W = 64
NA_KH = 8
NA_KW = 16
NA_COL_BLOCK = 16
NA_KEY_COLS = NA_COL_BLOCK + NA_KW
N_GROUPS = 4
EXPERTS_PER_GROUP = 8
N_EXPERTS = N_GROUPS * EXPERTS_PER_GROUP
TOP_K = 2
D_EXPERT = 512
ALPHA = (2 * DEPTH) ** 0.25
BETA = (8 * DEPTH) ** -0.25
N_A_LAYERS = (DEPTH + 1) // 2
N_B_LAYERS = DEPTH // 2
LN_EPS = 1e-5
NEG_INF = -1e30

kernel_name = "hybrid_dilated_neighbourhood_hmoe_encoder"

def layer_norm(x, g, b):
    xf = x.astype(jnp.float32)
    mu = jnp.mean(xf, axis=-1, keepdims=True)
    var = jnp.mean(jnp.square(xf - mu), axis=-1, keepdims=True)
    return ((xf - mu) * lax.rsqrt(var + LN_EPS) * g + b).astype(x.dtype)

def t5_bucket(rel):
    nb = N_BUCKETS // 2
    max_exact = nb // 2
    ret = jnp.where(rel > 0, nb, 0)
    n = jnp.abs(rel)
    nf = jnp.maximum(n, 1).astype(jnp.float32)
    large = max_exact + (jnp.log(nf / max_exact) / math.log(T5_MAX_DISTANCE / max_exact)
                         * (nb - max_exact)).astype(jnp.int32)
    large = jnp.minimum(large, nb - 1)
    return ret + jnp.where(n < max_exact, n, large)

def _dilated_branch(q, k, v, window, dilation, t5_table):
    B, S, H, Dh = q.shape
    half = window // (2 * dilation)
    L = S // dilation
    nblk = -(-L // DIL_BLOCK_Q)
    Lp = nblk * DIL_BLOCK_Q
    kw = DIL_BLOCK_Q + 2 * half

    def strided(a):
        return a.reshape(B, L, dilation, H, Dh).transpose(0, 2, 1, 3, 4)

    qs = jnp.pad(strided(q), ((0, 0), (0, 0), (0, Lp - L), (0, 0), (0, 0)))
    qs = qs.reshape(B, dilation, nblk, DIL_BLOCK_Q, H, Dh)
    pad_k = ((0, 0), (0, 0), (half, Lp - L + half), (0, 0), (0, 0))
    key_idx = np.arange(nblk)[:, None] * DIL_BLOCK_Q + np.arange(kw)[None, :]
    ks = jnp.take(jnp.pad(strided(k), pad_k), key_idx, axis=2)
    vs = jnp.take(jnp.pad(strided(v), pad_k), key_idx, axis=2)

    orig = key_idx - half
    valid = (orig >= 0) & (orig < L)
    rel = np.arange(kw)[None, :] - half - np.arange(DIL_BLOCK_Q)[:, None]
    band = np.abs(rel) <= half
    mask = band[None] & valid[:, None, :]
    bias = t5_table[t5_bucket(jnp.asarray(rel * dilation, dtype=jnp.int32))]
    bias = bias.transpose(2, 0, 1).astype(jnp.float32)

    s = jnp.einsum('bgnqhd,bgnkhd->bgnhqk', qs, ks).astype(jnp.float32) + bias
    s = jnp.where(mask[:, None], s, NEG_INF)
    lse = jax.nn.logsumexp(s, axis=-1)
    p = jnp.exp(s - lse[..., None]).astype(v.dtype)
    o = jnp.einsum('bgnhqk,bgnkhd->bgnqhd', p, vs)
    o = o.reshape(B, dilation, Lp, H, Dh)[:, :, :L].transpose(0, 2, 1, 3, 4).reshape(B, S, H, Dh)
    lse = lse.transpose(0, 1, 2, 4, 3).reshape(B, dilation, Lp, H)[:, :, :L]
    lse = lse.transpose(0, 2, 1, 3).reshape(B, S, H)
    return o, lse

def dilated_mixer(x, w_qkv, w_o, t5_table):
    B, S, _ = x.shape
    qkv = (x @ w_qkv).reshape(B, S, N_DIL, 3, N_HEADS_A, HEAD_DIM)
    outs, lses = [], []
    for g, (win, dil) in enumerate(DILATIONS):
        o, l = _dilated_branch(qkv[:, :, g, 0] * HEAD_DIM ** -0.5, qkv[:, :, g, 1],
                               qkv[:, :, g, 2], win, dil, t5_table)
        outs.append(o)
        lses.append(l)
    wts = jax.nn.softmax(jnp.stack(lses, 0), axis=0)
    o = jnp.einsum('gbsh,gbshd->bshd', wts, jnp.stack(outs, 0).astype(jnp.float32))
    return o.astype(x.dtype).reshape(B, S, N_HEADS_A * HEAD_DIM) @ w_o

def neighbourhood_mixer(x, w_qkv, w_o, rpb):
    B, S, _ = x.shape
    rows = S // GRID_W
    kh = min(NA_KH, rows)
    ncb = GRID_W // NA_COL_BLOCK
    H, Dh = N_HEADS_B, HEAD_DIM
    qkv = (x @ w_qkv).reshape(B, rows, GRID_W, 3, H, Dh)
    q = qkv[:, :, :, 0] * HEAD_DIM ** -0.5
    k = qkv[:, :, :, 1]
    v = qkv[:, :, :, 2]

    cols = np.arange(GRID_W)
    win_start = np.clip(cols - NA_KW // 2, 0, GRID_W - NA_KW)
    blk_start = np.clip(np.arange(ncb) * NA_COL_BLOCK - NA_KW // 2, 0, GRID_W - NA_KEY_COLS)
    key_cols = blk_start[:, None] + np.arange(NA_KEY_COLS)[None, :]
    q_cols = cols.reshape(ncb, NA_COL_BLOCK)
    ws = win_start[q_cols][:, :, None]
    kc = key_cols[:, None, :]
    col_mask = (kc >= ws) & (kc < ws + NA_KW)
    dc_idx = np.clip(kc - q_cols[:, :, None] + NA_KW - 1, 0, 2 * NA_KW - 2)

    k_cb = jnp.take(k, key_cols, axis=2)
    v_cb = jnp.take(v, key_cols, axis=2)

    def one_row(args):
        r, q_r = args
        rs = jnp.clip(r - kh // 2, 0, rows - kh)
        k_r = lax.dynamic_slice_in_dim(k_cb, rs, kh, axis=1)
        v_r = lax.dynamic_slice_in_dim(v_cb, rs, kh, axis=1)
        dr_idx = rs + jnp.arange(kh) - r + NA_KH - 1
        bias = jnp.take(jnp.take(rpb, dr_idx, axis=1), dc_idx, axis=2)
        bias = bias.transpose(2, 0, 3, 1, 4).astype(jnp.float32)
        s = jnp.einsum('bnqhd,binchd->bnhqic', q_r.reshape(B, ncb, NA_COL_BLOCK, H, Dh),
                       k_r).astype(jnp.float32) + bias
        s = jnp.where(col_mask[:, None, :, None, :], s, NEG_INF)
        p = jax.nn.softmax(s.reshape(B, ncb, H, NA_COL_BLOCK, kh * NA_KEY_COLS), axis=-1)
        p = p.reshape(s.shape).astype(v.dtype)
        o = jnp.einsum('bnhqic,binchd->bnqhd', p, v_r)
        return o.reshape(B, GRID_W, H, Dh)

    o = lax.map(one_row, (jnp.arange(rows), q.transpose(1, 0, 2, 3, 4)))
    o = o.transpose(1, 0, 2, 3, 4).reshape(B, S, H * Dh)
    return o @ w_o

def hierarchical_moe(x, w_rg, b_rg, w_re, b_re, w1, w3, w2):
    B, S, D = x.shape
    xf = x.reshape(-1, D)
    T = xf.shape[0]
    p_group = jax.nn.softmax((xf @ w_rg).astype(jnp.float32) + b_rg, axis=-1)
    g_sel = jnp.argmax(p_group, axis=-1)
    e_logits = ((xf @ w_re).astype(jnp.float32) + b_re).reshape(T, N_GROUPS, EXPERTS_PER_GROUP)
    e_in = jnp.take_along_axis(e_logits, g_sel[:, None, None], axis=1)[:, 0]
    top_v, top_i = lax.top_k(e_in, TOP_K)
    gate = jax.nn.softmax(top_v, axis=-1) * jnp.take_along_axis(p_group, g_sel[:, None], axis=1)
    eid = (g_sel[:, None] * EXPERTS_PER_GROUP + top_i).reshape(-1)
    tok = jnp.repeat(jnp.arange(T), TOP_K)
    order = jnp.argsort(eid)
    tok_s = tok[order]
    gate_s = gate.reshape(-1)[order]
    sizes = jnp.bincount(eid, length=N_EXPERTS).astype(jnp.int32)
    xs = xf[tok_s]
    h = jax.nn.silu(lax.ragged_dot(xs, w1, sizes)) * lax.ragged_dot(xs, w3, sizes)
    o = lax.ragged_dot(h, w2, sizes) * gate_s[:, None].astype(x.dtype)
    y = jnp.zeros_like(xf).at[tok_s].add(o)
    return y.reshape(B, S, D)

def _trunk(x, t5_table, w_qkv_a, w_o_a, w_qkv_b, w_o_b, rpb_b, ln_g, ln_b,
           w_rg, b_rg, w_re, b_re, w1, w3, w2):
    for i in range(DEPTH):
        j = i // N_MIXERS
        if i % N_MIXERS == 0:
            h = dilated_mixer(x, w_qkv_a[j], w_o_a[j], t5_table)
        else:
            h = neighbourhood_mixer(x, w_qkv_b[j], w_o_b[j], rpb_b[j])
        x = layer_norm(ALPHA * x + h, ln_g[i, 0], ln_b[i, 0])
        f = hierarchical_moe(x, w_rg[i], b_rg[i], w_re[i], b_re[i], w1[i], w3[i], w2[i])
        x = layer_norm(ALPHA * x + f, ln_g[i, 1], ln_b[i, 1])
    return x

def setup_inputs(seed: int = 0) -> dict:
    key = jax.random.key(seed)
    ks = jax.random.split(key, 17)
    f32 = jnp.float32

    def nrm(k, shape, scale):
        return jax.random.normal(k, shape, f32) * scale

    da = N_HEADS_A * HEAD_DIM
    db = N_HEADS_B * HEAD_DIM
    return {
        "x_prompt": nrm(ks[0], (BATCH, SEQ, D_MODEL), 1.0),
        "x_sample": nrm(ks[1], (DEC_BATCH, DEC_SEQ, D_MODEL), 1.0),
        "t5_table": nrm(ks[2], (N_BUCKETS, N_HEADS_A), 0.5),
        "w_qkv_a": nrm(ks[3], (N_A_LAYERS, D_MODEL, N_DIL * 3 * da), D_MODEL ** -0.5),
        "w_o_a": nrm(ks[4], (N_A_LAYERS, da, D_MODEL), BETA * da ** -0.5),
        "w_qkv_b": nrm(ks[5], (N_B_LAYERS, D_MODEL, 3 * db), D_MODEL ** -0.5),
        "w_o_b": nrm(ks[6], (N_B_LAYERS, db, D_MODEL), BETA * db ** -0.5),
        "rpb_b": nrm(ks[7], (N_B_LAYERS, N_HEADS_B, 2 * NA_KH - 1, 2 * NA_KW - 1), 0.5),
        "ln_g": 1.0 + nrm(ks[8], (DEPTH, 2, D_MODEL), 0.02),
        "ln_b": nrm(ks[9], (DEPTH, 2, D_MODEL), 0.02),
        "w_rg": nrm(ks[10], (DEPTH, D_MODEL, N_GROUPS), D_MODEL ** -0.5),
        "b_rg": nrm(ks[11], (DEPTH, N_GROUPS), 0.01),
        "w_re": nrm(ks[12], (DEPTH, D_MODEL, N_EXPERTS), D_MODEL ** -0.5),
        "b_re": nrm(ks[13], (DEPTH, N_EXPERTS), 0.01),
        "w1": nrm(ks[14], (DEPTH, N_EXPERTS, D_MODEL, D_EXPERT), D_MODEL ** -0.5),
        "w3": nrm(ks[15], (DEPTH, N_EXPERTS, D_MODEL, D_EXPERT), D_MODEL ** -0.5),
        "w2": nrm(ks[16], (DEPTH, N_EXPERTS, D_EXPERT, D_MODEL), BETA * D_EXPERT ** -0.5),
    }

def reference(x_prompt, x_sample, t5_table, w_qkv_a, w_o_a, w_qkv_b, w_o_b, rpb_b,
              ln_g, ln_b, w_rg, b_rg, w_re, b_re, w1, w3, w2):
    y_prompt = _trunk(x_prompt, t5_table, w_qkv_a, w_o_a, w_qkv_b, w_o_b, rpb_b, ln_g, ln_b,
                      w_rg, b_rg, w_re, b_re, w1, w3, w2)
    y_sample = _trunk(x_sample, t5_table, w_qkv_a, w_o_a, w_qkv_b, w_o_b, rpb_b, ln_g, ln_b,
                      w_rg, b_rg, w_re, b_re, w1, w3, w2)
    return (y_prompt, y_sample)


_drawn_inputs = setup_inputs


def setup_inputs(seed=0):
    import zlib

    import numpy as np

    out = dict(_drawn_inputs(seed))
    spreads = {}
    factors = {'t5_table': 2.685, 'b_rg': 7.175, 'b_re': 6.652}
    for name, (base, spread) in spreads.items():
        noise = np.random.default_rng([zlib.crc32(name.encode()), seed]).standard_normal(out[name].shape)
        drawn = base * np.exp(spread * noise) if base else spread * noise
        out[name] = __import__('jax').numpy.asarray(drawn.astype(out[name].dtype))
    for name, factor in factors.items():
        out[name] = (out[name] * factor).astype(out[name].dtype)
    return out
```

```python
from contextlib import ExitStack, contextmanager
import math

import numpy as np

import concourse.bass as bass
from concourse import mybir

F32 = mybir.dt.float32
F32R = mybir.dt.float32r
BF16 = mybir.dt.bfloat16
I32 = mybir.dt.int32
U32 = mybir.dt.uint32
ALU = mybir.AluOpType
ACT = mybir.ActivationFunctionType
AX = mybir.AxisListType

P = 128
D = 1024
KC = D // P
N_SEQ = 2
SEQ = 1024
TOKENS = N_SEQ * SEQ
TILES = TOKENS // P
SEQ_TILES = SEQ // P
HALF = 512
HEADS = 16
HD = 64
PAIRS = HEADS // 2
DILATIONS = (1, 4, 16)
N_DIL = len(DILATIONS)
REACH = 64
N_BUCKETS = 32
T5_MAX_DISTANCE = 1024
GRID_W = 64
GRID_H = SEQ // GRID_W
NA_KH = 8
NA_KW = 16
N_GROUPS = 4
PER_GROUP = 8
N_EXPERTS = N_GROUPS * PER_GROUP
TOP_K = 2
D_EXPERT = 512
DEPTH = 2
ALPHA = (2 * DEPTH) ** 0.25
LN_EPS = 1e-5
NEG = -1e30
BIG = 3e38
OROW = 2 * HD + 4

BLOCKS = (TOKENS * TOP_K - N_EXPERTS) // P + N_EXPERTS
SLOTS = (BLOCKS + 1) * P
MAX_BLOCKS_OF_ONE = TOKENS // P
EXPERT_PIECES = 12
W13_PIECES = 8
W2_PIECES = 4


REL = 255
REL_ROW = 2 * REL + 2
N_ROW = N_DIL * REL_ROW


def t5_bucket(rel):
    nb = N_BUCKETS // 2
    max_exact = nb // 2
    ret = np.where(rel > 0, nb, 0)
    n = np.abs(rel)
    nf = np.maximum(n, 1).astype(np.float32)
    large = max_exact + (np.log(nf / np.float32(max_exact)) / np.float32(math.log(T5_MAX_DISTANCE / max_exact))
                         * np.float32(nb - max_exact)).astype(np.int32)
    large = np.minimum(large, nb - 1)
    return ret + np.where(n < max_exact, n, large)


def bucket_select():
    sel = np.zeros((N_BUCKETS + 1, N_DIL, REL_ROW), np.float32)
    rel = np.arange(REL_ROW) - REL
    inside = np.abs(rel) <= REACH
    for g, dil in enumerate(DILATIONS):
        row = np.where(inside, t5_bucket(rel * dil), N_BUCKETS)
        if g == 2:
            row = np.where((rel % 2 == 0) & (np.abs(rel) <= 2 * REACH), t5_bucket(rel * dil // 2), N_BUCKETS)
        sel[row, g, np.arange(REL_ROW)] = 1.0
    return sel.reshape(N_BUCKETS + 1, N_ROW)


NA_T0 = -6
NA_TN = 14
IN_T0 = -4
IN_TN = 10


def grid_masks():
    q = np.arange(P)
    row, col = q // GRID_W, q % GRID_W
    start = np.clip(col - NA_KW // 2, 0, GRID_W - NA_KW)
    kc = np.arange(GRID_W)
    cols = (kc[None] >= start[:, None]) & (kc[None] < start[:, None] + NA_KW)
    edge = np.where(cols, 0.0, NEG).astype(np.float32)
    t = np.arange(IN_TN) + IN_T0
    rows = (t[None] >= row[:, None] - NA_KH // 2) & (t[None] < row[:, None] + NA_KH // 2)
    inner = np.where(rows[:, :, None] & cols[:, None, :], 0.0, NEG).astype(np.float32)
    return edge, inner.reshape(P, IN_TN * GRID_W)


def grid_tiles():
    out = []
    for i in range(GRID_H // 2):
        lo = min(max(2 * i - NA_KH // 2, 0), GRID_H - NA_KH)
        hi = min(max(2 * i + 1 - NA_KH // 2, 0), GRID_H - NA_KH) + NA_KH
        c0, c1 = lo // 2, (hi + 1) // 2
        moves = hi - lo > NA_KH
        out.append((c0, c1 - c0, moves, 2 * c0 - 2 * i - (IN_T0 if moves else NA_T0)))
    return out


def small_constants():
    p = np.arange(P)
    return {
        "c_bucket": bucket_select(),
        "c_edge": grid_masks()[0],
        "c_inner": grid_masks()[1],
        "c_ident": np.eye(P, dtype=np.float32),
        "c_before": (p[:, None] < p[None, :]).astype(np.float32),
        "c_iota": np.broadcast_to(np.arange(BLOCKS + 1, dtype=np.float32), (P, BLOCKS + 1)).copy(),
    }


class Scratch:

    def __init__(self, nc):
        def dram(name, shape):
            return nc.dram_tensor(name, shape, F32, kind="Internal").ap()

        self.bias_rows = dram("bias_rows", (HEADS, N_ROW))
        self.bias_a = dram("bias_a", (HEADS, P, B_COLS))
        self.rpb_rows = dram("rpb_rows", (HEADS * (2 * NA_KH - 1), 2 * GRID_W - 1))
        self.rpb_raw = dram("rpb_raw", (HEADS, P, NA_TN * GRID_W))
        self.bias_b = dram("bias_b", (HEADS, P, (NA_TN + IN_TN) * GRID_W))
        self.qT = dram("qT", (N_SEQ * N_DIL, D, SEQ))
        self.kT = dram("kT", (N_SEQ * N_DIL, D, SEQ))
        self.v = dram("v", (N_SEQ * N_DIL, SEQ, D))
        self.o = dram("o", (N_DIL, TOKENS, PAIRS * OROW))
        self.x1 = dram("x1", (TOKENS, D))
        self.x2 = dram("x2", (TOKENS, D))
        self.xs = dram("xs", (SLOTS, D))
        self.ys = dram("ys", (SLOTS, D))


@contextmanager
def phase_semaphores(nc, tag):
    taken = []

    def sem(name):
        taken.append(nc.alloc_semaphore(f"{tag}_{name}"))
        return taken[-1]

    yield sem
    nc.clear_and_free_semaphores(taken)
    nc.all_engine_barrier()


def project_qkv(nc, tag, x, w, ident, n_g, qT, kT, v, clear=()):
    with ExitStack() as ctx:
        def sb(name, shape, dt=F32):
            return ctx.enter_context(nc.sbuf_tensor(f"{tag}_{name}", shape, dt))

        sem = ctx.enter_context(phase_semaphores(nc, tag))

        GROUPS = 6
        OUTS = 8
        KINDS = [(kind, half) for half in range(2) for kind in range(3)]
        W_PARTS = 4
        WK = KC // W_PARTS
        BANKS = 4

        x_rows = sb("x_rows", [P, 2, D])
        xT_hi = sb("xT_hi", [P, KC, SEQ], F32R)
        xT_lo = sb("xT_lo", [P, KC, SEQ], F32R)
        w_raw = sb("w_raw", [P, 2, KC, HALF])
        w_hi = sb("w_hi", [P, 2, KC, HALF], F32R)
        w_lo = sb("w_lo", [P, 2, KC, HALF], F32R)
        stage = sb("stage", [P, BANKS, HALF])
        ps_x = ctx.enter_context(nc.psum_tensor(f"{tag}_ps_x", [P, 2, 4, P], F32))
        ps_out = ctx.enter_context(nc.psum_tensor(f"{tag}_ps_out", [P, BANKS, HALF], F32))

        x_loaded = [sem(f"x_loaded{i}") for i in range(2)]
        w_loaded = [sem(f"w_loaded{i}") for i in range(2)]
        x_turned = sem("x_turned")
        x_hi_done = sem("x_hi_done")
        x_lo_done = sem("x_lo_done")
        w_hi_done = sem("w_hi_done")
        w_lo_done = sem("w_lo_done")
        out_done = sem("out_done")
        stage_full = sem("stage_full")
        stored = [sem(f"stored{i}") for i in range(BANKS)]

        zeros = sb("zeros", [P, D]) if clear else None
        zeroed, cleared = sem("zeroed"), sem("cleared")

        with nc.Block() as block:
            @block.gpsimd
            def _(pool):
                if clear:
                    pool.memset(zeros[:], 0.0).then_inc(zeroed, 1)
                    pool.wait_ge(zeroed, 1)
                    for r, rows in enumerate(clear):
                        for i in range(SLOTS // P):
                            pool.wait_ge(out_done, 2 * OUTS + r * (SLOTS // P) + i + 1)
                            pool.dma_start(rows[bass.ts(i, P), :], zeros[:]).then_inc(cleared, 16)
                    pool.wait_ge(cleared, 16 * len(clear) * (SLOTS // P))

            @block.sync
            def _(sp):
                with sp.Fori(0, N_SEQ) as s:
                    for t in range(SEQ_TILES):
                        sp.wait_ge(x_turned, 2 * (s * SEQ_TILES + t) + 2)
                        sp.dma_start(x_rows[:, t % 2, :], x[bass.ds(s * SEQ + t * P, P), :]
                                     ).then_inc(x_loaded[t % 2], 16)
                    with sp.Fori(0, n_g) as g:
                        for c, (kind, half) in enumerate(KINDS):
                            n = (s * n_g + g) * GROUPS + c
                            sp.wait_ge(w_lo_done, W_PARTS * (n + 1))
                            col = g * (3 * D) + (kind * D + half * HALF)
                            sp.dma_start(w_raw[:, c % 2], w[:, bass.ds(col, HALF)].rearrange(
                                "(k p) n -> p k n", p=P)).then_inc(w_loaded[c % 2], 16)

            @block.tensor
            def _(pe):
                pe.sem_inc(x_turned, 4)
                pe.sem_inc(out_done, 2 * OUTS)
                with pe.Fori(0, N_SEQ) as s:
                    for t in range(SEQ_TILES):
                        pe.wait_ge(x_loaded[t % 2], 16 * (s * (SEQ_TILES // 2) + t // 2 + 1))
                        for h in range(2):
                            pe.wait_ge(x_lo_done, 2 * (s * SEQ_TILES + t) + h + 1)
                            for k in range(4):
                                done = pe.transpose(ps_x[:, h, k, :], x_rows[:, t % 2, bass.ts(4 * h + k, P)],
                                                    ident[:])
                            done.then_inc(x_turned, 1)
                    with pe.Fori(0, n_g) as g:
                        pe.wait_ge(x_lo_done, 2 * SEQ_TILES * (s + 1) + 2)
                        for c, (kind, half) in enumerate(KINDS):
                            n = (s * n_g + g) * GROUPS + c
                            pe.wait_ge(w_lo_done, W_PARTS * (n + 3))
                            for j in range(OUTS):
                                pe.wait_ge(stage_full, n * OUTS + j + 1)
                                first = True
                                for k in range(KC):
                                    if kind < 2:
                                        wcols, toks = bass.ts(j // 2, P), bass.ts(j % 2, HALF)
                                        parts = ((w_hi[:, c % 2, k, wcols], xT_hi[:, k, toks]),
                                                 (w_hi[:, c % 2, k, wcols], xT_lo[:, k, toks]),
                                                 (w_lo[:, c % 2, k, wcols], xT_hi[:, k, toks]))
                                    else:
                                        toks = bass.ts(j, P)
                                        parts = ((xT_hi[:, k, toks], w_hi[:, c % 2, k, :]),
                                                 (xT_hi[:, k, toks], w_lo[:, c % 2, k, :]),
                                                 (xT_lo[:, k, toks], w_hi[:, c % 2, k, :]))
                                    for m, (stationary, moving) in enumerate(parts):
                                        done = pe.matmul(ps_out[:, j % BANKS, :], stationary, moving, start=first,
                                                         stop=(k == KC - 1 and m == 2))
                                        first = False
                                done.then_inc(out_done, 1)

            @block.scalar
            def _(act):
                act.sem_inc(stage_full, BANKS)
                for i in range(BANKS):
                    act.sem_inc(stored[i], 16)
                with act.Fori(0, N_SEQ) as s:
                    act.wait_ge(out_done, s * (n_g * GROUPS * OUTS) + 2 * OUTS)
                    for t in range(SEQ_TILES):
                        for h in range(2):
                            act.wait_ge(x_turned, 2 * (s * SEQ_TILES + t) + h + 5)
                            act.activation(xT_hi[:, 4 * h:4 * h + 4, bass.ts(t, P)], ps_x[:, h], ACT.Copy
                                           ).then_inc(x_hi_done, 1)
                    with act.Fori(0, n_g) as g:
                        for c, (kind, half) in enumerate(KINDS):
                            sg = s * n_g + g
                            n = sg * GROUPS + c
                            for j in range(OUTS):
                                act.wait_ge(out_done, (n + 2) * OUTS + j + 1)
                                act.wait_ge(stored[j % BANKS], 16 * (n * (OUTS // BANKS) + j // BANKS + 1))
                                act.activation(stage[:, j % BANKS, :], ps_out[:, j % BANKS, :], ACT.Copy,
                                               scale=HD ** -0.5 if kind == 0 else 1.0).then_inc(stage_full, 1)
                                act.wait_ge(stage_full, n * OUTS + j + 1 + BANKS)
                                if kind < 2:
                                    dst = (qT, kT)[kind][bass.ds(sg, 1), half * HALF + (j // 2) * P:
                                                         half * HALF + (j // 2 + 1) * P, bass.ts(j % 2, HALF)]
                                else:
                                    dst = v[bass.ds(sg, 1), bass.ts(j, P), bass.ts(half, HALF)]
                                act.dma_start(dst.rearrange("a p n -> p (a n)"), stage[:, j % BANKS, :]
                                              ).then_inc(stored[j % BANKS], 16)
                for i in range(BANKS):
                    act.wait_ge(stored[i], 16 * (N_SEQ * n_g * GROUPS * OUTS // BANKS + 1))

            @block.vector
            def _(dve):
                dve.sem_inc(x_lo_done, 2)
                dve.sem_inc(w_lo_done, 2 * W_PARTS)
                with dve.Fori(0, N_SEQ) as s:
                    for t in range(SEQ_TILES):
                        for h in range(2):
                            dve.wait_ge(x_hi_done, 2 * (s * SEQ_TILES + t) + h + 1)
                            tile = (slice(None), slice(4 * h, 4 * h + 4), bass.ts(t, P))
                            dve.tensor_tensor(xT_lo[tile], ps_x[:, h], xT_hi[tile].bitcast(F32), ALU.subtract
                                              ).then_inc(x_lo_done, 1)
                    with dve.Fori(0, n_g) as g:
                        for c in range(GROUPS):
                            n = (s * n_g + g) * GROUPS + c
                            dve.wait_ge(w_loaded[c % 2], 16 * ((s * n_g + g) * (GROUPS // 2) + c // 2 + 1))
                            dve.wait_ge(out_done, (n + 1) * OUTS)
                            for i in range(W_PARTS):
                                ks = slice(WK * i, WK * i + WK)
                                dve.tensor_copy(w_hi[:, c % 2, ks], w_raw[:, c % 2, ks]).then_inc(w_hi_done, 1)
                            for i in range(W_PARTS):
                                ks = slice(WK * i, WK * i + WK)
                                dve.wait_ge(w_hi_done, W_PARTS * n + i + 1)
                                dve.tensor_tensor(w_lo[:, c % 2, ks], w_raw[:, c % 2, ks],
                                                  w_hi[:, c % 2, ks].bitcast(F32), ALU.subtract
                                                  ).then_inc(w_lo_done, 1)


def strided(start, count, step):
    return slice(start, start + step * (count - 1) + 1, step)


KEYS = 2 * P
B_COLS = 3 * KEYS + 2 * KEYS + P


def diagonal_tiles():
    every = slice(0, P)
    masked = REL - REACH - HD
    out = [(every, slice(0, REACH), 0, masked), (every, slice(REACH, KEYS), 0, REL),
           (every, slice(KEYS, 2 * KEYS), 0, REL - REACH),
           (every, slice(2 * KEYS, 3 * KEYS - REACH), 0, REL - REACH),
           (every, slice(3 * KEYS - REACH, 3 * KEYS), 0, masked)]
    for u in range(2):
        out.append((every, slice((3 + u) * KEYS, (4 + u) * KEYS), 1, REL - P * u))
    out.append((every, slice(5 * KEYS, 5 * KEYS + P), 2, REL))
    return out


def bias_rows(nc, t5_table, c_bucket, scratch):
    with ExitStack() as ctx:
        sem = ctx.enter_context(phase_semaphores(nc, "br"))
        table = ctx.enter_context(nc.sbuf_tensor("br_table", [N_BUCKETS + 1, HEADS], F32))
        select = ctx.enter_context(nc.sbuf_tensor("br_select", [N_BUCKETS + 1, N_ROW], F32))
        rows = ctx.enter_context(nc.sbuf_tensor("br_rows", [HEADS, N_ROW], F32))
        ps = ctx.enter_context(nc.psum_tensor("br_ps", [P, N_DIL, REL_ROW], F32))
        loaded, masked, made, copied, stored = (sem(n) for n in (
            "loaded", "masked", "made", "copied", "stored"))
        with nc.Block() as block:
            @block.sync
            def _(sp):
                sp.dma_start(select[:], c_bucket).then_inc(loaded, 16)
                sp.dma_start(table[0:N_BUCKETS, :], t5_table).then_inc(loaded, 16)
                sp.wait_ge(copied, N_DIL)
                sp.dma_start(scratch.bias_rows, rows[:]).then_inc(stored, 16)
                sp.wait_ge(stored, 16)
                tiles = diagonal_tiles()
                for part, cols, g, shift in tiles:
                    src = bass.AP(scratch.bias_rows.tensor, g * REL_ROW + shift,
                                  [[N_ROW, HEADS], [-1, part.stop - part.start], [1, cols.stop - cols.start]])
                    sp.dma_start(scratch.bias_a[:, part, cols], src).then_inc(stored, 16)
                sp.wait_ge(stored, 16 * (len(tiles) + 1))

            @block.vector
            def _(dve):
                dve.memset(table[N_BUCKETS:N_BUCKETS + 1, :], NEG).then_inc(masked, 1)
                for g in range(N_DIL):
                    dve.wait_ge(made, g + 1)
                    dve.tensor_copy(rows[:, bass.ts(g, REL_ROW)], ps[0:HEADS, g, :]).then_inc(copied, 1)

            @block.tensor
            def _(pe):
                pe.wait_ge(loaded, 32)
                pe.wait_ge(masked, 1)
                for g in range(N_DIL):
                    pe.matmul(ps[0:HEADS, g, :], table[:], select[:, bass.ts(g, REL_ROW)], start=True, stop=True
                              ).then_inc(made, 1)


def dilated_attention(nc, ident, scratch):
    K_PAD = SEQ + 2 * REACH
    CHUNKS = (SEQ_TILES + 1, SEQ_TILES, SEQ_TILES)
    V0 = (0, CHUNKS[0], CHUNKS[0] + CHUNKS[1])
    jobs = []
    for t in range(SEQ_TILES):
        col = 0 if t == 0 else 2 * KEYS if t == SEQ_TILES - 1 else KEYS
        jobs.append(dict(g=0, t=t, nk=KEYS, bias=col, chunk=V0[0] + t,
                         q=bass.ts(t, P), k=slice(t * P, t * P + KEYS)))
    for t in range(SEQ_TILES):
        r, half = t // 2, t % 2
        jobs.append(dict(g=1, t=t, nk=KEYS, bias=(3 + half) * KEYS, chunk=V0[1] + 2 * r,
                         q=strided(4 * P * half + r, P, 4), k=strided(r, KEYS, 4)))
    for t in range(SEQ_TILES):
        jobs.append(dict(g=2, t=t, nk=P, bias=5 * KEYS, chunk=V0[2] + t,
                         q=strided(t, P, 8), k=strided(t, P, 8)))
    JOBS = len(jobs)

    with ExitStack() as ctx:
        def sb(name, shape, dt=F32):
            return ctx.enter_context(nc.sbuf_tensor(f"da_{name}", shape, dt))

        sem = ctx.enter_context(phase_semaphores(nc, "da"))

        q_one = sb("q_one", [P, 2, N_DIL, 2, SEQ])
        k_two = sb("k_two", [P, 2, N_DIL, K_PAD])
        v_two = sb("v_two", [P, 2, sum(CHUNKS), P])
        bias = sb("bias", [P, 2, 2, B_COLS])
        minus_s = sb("minus_s", [P, 2, 2, KEYS])
        prob = sb("prob", [P, 2, 2, KEYS])
        probT = sb("probT", [P, 2, 4, P])
        rows = sb("rows", [P, 2, JOBS, OROW])
        ps_s = ctx.enter_context(nc.psum_tensor("da_ps_s", [P, 2, 2, KEYS], F32))
        ps_t = ctx.enter_context(nc.psum_tensor("da_ps_t", [P, 2, 4, P], F32))
        ps_o = ctx.enter_context(nc.psum_tensor("da_ps_o", [P, 2, 4, P], F32))

        zeroed = sem("zeroed")
        q_zeroed = sem("q_zeroed")
        loaded = [sem(f"loaded{i}") for i in range(2)]
        scored = sem("scored")
        biased = sem("biased")
        exped = sem("exped")
        turned = sem("turned")
        turned_sb = sem("turned_sb")
        summed = sem("summed")
        stepped = sem("stepped")
        placed = sem("placed")
        stored = [sem(f"stored{i}") for i in range(2)]

        with nc.Block() as block:
            def loads(slot, hp):
                s = slot
                ch = hp * P
                out = []
                q = scratch.qT[s * N_DIL:(s + 1) * N_DIL]
                k = scratch.kT[s * N_DIL:(s + 1) * N_DIL, bass.ds(ch, P), :].rearrange("g c t -> c g t")
                for head in range(2):
                    rng = slice(HD * head, HD * head + HD)
                    out.append((q_one[rng, slot, :, head, :],
                                q[:, bass.ds(ch + HD * head, HD), :].rearrange("g c t -> c g t")))
                out.append((k_two[:, slot, 0, REACH:REACH + SEQ], k[:, 0, :]))
                out.append((k_two[:, slot, 1:3, 0:SEQ], k[:, 1:3, :]))
                v = scratch.v
                v0 = v[s * N_DIL, :, bass.ds(ch, P)].rearrange("(c u p) n -> u p c n", u=2, p=HD)
                out.append((v_two[HD:P, slot, 0:SEQ_TILES, :], v0[0]))
                out.append((v_two[0:HD, slot, 1:SEQ_TILES + 1, :], v0[1]))
                v1 = v[s * N_DIL + 1, :, bass.ds(ch, P)].rearrange("(u p r) n -> r p u n", u=2, r=4)
                for r in range(4):
                    out.append((v_two[:, slot, V0[1] + 2 * r:V0[1] + 2 * r + 2, :], v1[r]))
                v2 = v[s * N_DIL + 2, :, bass.ds(ch, P)].rearrange("(p t) n -> p t n", t=8)
                out.append((v_two[:, slot, V0[2]:V0[2] + 8, :], v2))
                out.append((bias[:, slot], scratch.bias_a[bass.ds(2 * hp, 2)].rearrange("h p n -> p h n")))
                return out

            N_LOAD = len(loads(0, 0))

            def out_rows(slot, hp, g):
                o = scratch.o[g, bass.ts(slot, SEQ), bass.ds(hp * OROW, OROW)]
                src = rows[:, slot, bass.ts(g, SEQ_TILES), :]
                if g == 0:
                    return [(o.rearrange("(t p) n -> p t n", p=P), src)]
                if g == 1:
                    o = o.rearrange("(u p r) n -> r p u n", u=2, r=4)
                    return [(o[r], src[:, 2 * r:2 * r + 2, :]) for r in range(4)]
                return [(o.rearrange("(p t) n -> p t n", t=8), src)]

            N_STORE = sum(len(out_rows(0, 0, g)) for g in range(N_DIL))

            @block.sync
            def _(sp):
                sp.wait_ge(zeroed, 4)
                sp.wait_ge(q_zeroed, 2)
                with sp.Fori(0, PAIRS) as hp:
                    for s in range(N_SEQ):
                        sp.wait_ge(summed, (2 * hp + s + 1) * JOBS)
                        for dst, src in loads(s, hp):
                            sp.dma_start(dst, src).then_inc(loaded[s], 16)

            @block.gpsimd
            def _(pool):
                for i, pad in enumerate((k_two[:, :, 0, 0:REACH], k_two[:, :, 0, REACH + SEQ:K_PAD],
                                         v_two[0:HD, :, 0, :], v_two[HD:P, :, SEQ_TILES, :])):
                    if i:
                        pool.wait_ge(zeroed, i)
                    pool.memset(pad, 0.0).then_inc(zeroed, 1)

            body = [(s, n, job) for s in range(N_SEQ) for n, job in enumerate(jobs)]
            ALL = len(body)

            @block.tensor
            def _(pe):
                pe.sem_inc(turned, 2)
                pe.sem_inc(summed, 2 * JOBS)
                with pe.Fori(0, PAIRS) as hp:
                    base = hp * ALL

                    def scores(j):
                        s, n, job = body[j]
                        if n == 0:
                            pe.wait_ge(loaded[s], 16 * N_LOAD * (hp + 1))
                        pe.wait_ge(biased, 2 * (base + j) + 2)
                        for head in range(2):
                            done = pe.matmul(ps_s[:, j % 2, head, 0:job["nk"]],
                                             q_one[:, s, job["g"], head, job["q"]],
                                             k_two[:, s, job["g"], job["k"]], start=True, stop=True)
                        done.then_inc(scored, 1)

                    def transposes(j):
                        s, n, job = body[j]
                        pe.wait_ge(exped, 2 * (base + j) + 2)
                        pe.wait_ge(turned_sb, base + j + 1)
                        nc_ = job["nk"] // P
                        for head in range(2):
                            for c in range(nc_):
                                done = pe.transpose(ps_t[:, j % 2, head * nc_ + c, :],
                                                    prob[:, j % 2, head, bass.ts(c, P)], ident[:])
                        done.then_inc(turned, 1)

                    def outputs(j):
                        s, n, job = body[j]
                        pe.wait_ge(turned_sb, base + j + 3)
                        pe.wait_ge(placed, base + j + 1)
                        nc_ = job["nk"] // P
                        for head in range(2):
                            for c in range(nc_):
                                done = pe.matmul(ps_o[:, j % 2, head, :], probT[:, j % 2, head * nc_ + c, :],
                                                 v_two[:, s, job["chunk"] + c, :], start=(c == 0),
                                                 stop=(c == nc_ - 1))
                        done.then_inc(summed, 1)

                    scores(0)
                    scores(1)
                    for j in range(ALL):
                        transposes(j)
                        if j + 2 < ALL:
                            scores(j + 2)
                        if j >= 1:
                            outputs(j - 1)
                    outputs(ALL - 1)

            @block.vector
            def _(dve):
                dve.sem_inc(biased, 4)
                dve.sem_inc(placed, 2)
                dve.memset(q_one[0:HD, :, :, 1, :], 0.0).then_inc(q_zeroed, 1)
                dve.memset(q_one[HD:P, :, :, 0, :], 0.0).then_inc(q_zeroed, 1)
                with dve.Fori(0, PAIRS) as hp:
                    base = hp * ALL

                    def add_bias(j):
                        s, n, job = body[j]
                        if n == 0:
                            dve.wait_ge(loaded[s], 16 * N_LOAD * (hp + 1))
                            dve.wait_ge(stored[s], 16 * N_STORE * (hp + 1))
                        dve.wait_ge(scored, base + j + 1)
                        dve.wait_ge(turned, base + j + 1)
                        dve.sem_inc(stepped, 1)
                        nk, col = job["nk"], job["bias"]
                        for head in range(2):
                            dve.tensor_tensor_reduce(
                                minus_s[:, j % 2, head, 0:nk], ps_s[:, j % 2, head, 0:nk],
                                bias[:, s, head, col:col + nk], -1.0, BIG, ALU.add, ALU.min,
                                rows[:, s, n, 2 * HD + 2 * head:2 * HD + 2 * head + 1]).then_inc(biased, 1)

                    def place(j):
                        s, n, job = body[j]
                        dve.wait_ge(summed, base + j + 1 + 2 * JOBS)
                        own = ps_o[:, j % 2, 0:3, :].rearrange("p a n -> p (a n)").rearrange(
                            "p (h x) -> p h x", h=2)[:, :, 0:HD]
                        dve.tensor_copy(rows[:, s, n, 0:2 * HD].rearrange("p (h x) -> p h x", h=2), own
                                        ).then_inc(placed, 1)

                    for j in range(ALL):
                        add_bias(j)
                        if j >= 3:
                            place(j - 3)
                    for j in range(ALL - 3, ALL):
                        place(j)

            @block.scalar
            def _(act):
                act.sem_inc(turned_sb, 2)
                for s in range(N_SEQ):
                    act.sem_inc(stored[s], 16 * N_STORE)
                with act.Fori(0, PAIRS) as hp:
                    base = hp * ALL

                    def store(s, g):
                        act.wait_ge(placed, (2 * hp + s) * JOBS + (g + 1) * SEQ_TILES + 2)
                        for dst, src in out_rows(s, hp, g):
                            act.dma_start(dst, src).then_inc(stored[s], 16)

                    def exps(j):
                        s, n, job = body[j]
                        for head in range(2):
                            act.wait_ge(biased, 2 * (base + j) + head + 5)
                            if head == 0:
                                act.wait_ge(turned, base + j + 1)
                            at = 2 * HD + 2 * head
                            act.activation(prob[:, j % 2, head, 0:job["nk"]], minus_s[:, j % 2, head, 0:job["nk"]],
                                           ACT.Exp, bias=rows[:, s, n, at:at + 1], scale=-1.0,
                                           accum_out=rows[:, s, n, at + 1:at + 2]).then_inc(exped, 1)

                    def copy(j):
                        s, n, job = body[j]
                        act.wait_ge(turned, base + j + 3)
                        act.wait_ge(summed, base + j - 1 + 2 * JOBS)
                        m = 2 * job["nk"] // P
                        act.activation(probT[:, j % 2, 0:m, :], ps_t[:, j % 2, 0:m, :], ACT.Copy
                                       ).then_inc(turned_sb, 1)

                    for j in range(ALL):
                        exps(j)
                        if j >= 1:
                            copy(j - 1)
                        if j >= SEQ_TILES + 5 and (j - 5) % SEQ_TILES == 0:
                            store(*divmod((j - 5) // SEQ_TILES - 1, N_DIL))
                    copy(ALL - 1)
                    store(N_SEQ - 1, N_DIL - 1)
                for s in range(N_SEQ):
                    act.wait_ge(stored[s], 16 * N_STORE * (PAIRS + 1))


def staged(eng, count, steps):
    most = max(lag for lag, _ in steps)
    first = most + (count - most) % 2

    def turn(n):
        for lag, fn in steps:
            if 0 <= n - lag < count:
                fn(n - lag, (n - lag) % 2)

    for n in range(first):
        turn(n)
    with eng.Fori(0, (count - first) // 2) as i:
        for w in range(2):
            for lag, fn in steps:
                fn(2 * i + (first + w - lag), (first + w - lag) % 2)
    for n in range(count, count + most):
        turn(n)


def rounds(t, u):
    return t // 2 + 1 if isinstance(t, int) else (t - u) // 2 + 1


def first(t):
    return isinstance(t, int) and t == 0


def row_broadcast(row):
    return bass.AP(row.tensor, row.offset, [[0, P], [1, row.shape[-1]]])


def merge_and_norm(nc, tag, n_g, x, w_o, gain, shift, w_rg, b_rg, w_re, b_re, ident, logits, scratch):
    N_LOGITS = N_GROUPS + N_EXPERTS
    MIX = 5 if n_g > 1 else 1
    NORM = 8
    with ExitStack() as ctx:
        def sb(name, shape, dt=F32):
            return ctx.enter_context(nc.sbuf_tensor(f"{tag}_{name}", shape, dt))

        def ps(name, shape):
            return ctx.enter_context(nc.psum_tensor(f"{tag}_{name}", shape, F32))

        sem = ctx.enter_context(phase_semaphores(nc, tag))

        w_raw = sb("w_raw", [P, 2, D])
        wo_hi = sb("wo_hi", [P, KC, D], F32R)
        wo_lo = sb("wo_lo", [P, KC, D], F32R)
        wr = sb("wr", [P, KC, P])
        br = sb("br", [P, N_LOGITS])
        gain_sb = sb("gain", [P, D])
        shift_sb = sb("shift", [P, D])
        o_in = sb("o_in", [P, 2, n_g, PAIRS * OROW])
        x_in = sb("x_in", [P, 2, D])
        low = sb("low", [P, HEADS])
        gap = sb("gap", [P, n_g, HEADS])
        part = sb("part", [P, n_g, HEADS])
        mass = sb("mass", [P, n_g, HEADS])
        total = sb("total", [P, HEADS])
        inverse = sb("inverse", [P, HEADS])
        weight = sb("weight", [P, n_g, HEADS])
        merged = sb("merged", [P, D])
        oT_hi = sb("oT_hi", [P, 2, KC, P], F32R)
        oT_lo = sb("oT_lo", [P, 2, KC, P], F32R)
        res = sb("res", [P, D])
        stats = sb("stats", [P, 2, 6])
        mean_var = sb("mean_var", [P, 2, 2])
        power = sb("power", [P, 1])
        guess = sb("guess", [P, 2, 1])
        check = sb("check", [P, 1])
        fix = sb("fix", [P, 1])
        rstd = sb("rstd", [P, 1])
        x1 = sb("x1", [P, 2, D])
        x1T = sb("x1T", [P, KC, P])
        ps_o = ps("ps_o", [P, 2, 4, P])
        ps_x = ps("ps_x", [P, 2, 4, P])
        ps_h = ps("ps_h", [P, 2, HALF])
        ps_l = ps("ps_l", [P, P])

        w_loaded = [sem(f"w_loaded{i}") for i in range(2)]
        const_loaded = sem("const_loaded")
        o_loaded = [sem(f"o_loaded{i}") for i in range(2)]
        x_loaded = [sem(f"x_loaded{i}") for i in range(2)]
        padded = sem("padded")
        wo_hi_done = sem("wo_hi_done")
        wo_lo_done = sem("wo_lo_done")
        mix = sem("mix")
        small = sem("small")
        stepped = sem("stepped")
        outer = sem("outer")
        exped = sem("exped")
        middle = sem("middle")
        merges = sem("merges")
        o_turned = sem("o_turned")
        o_hi = sem("o_hi")
        o_lo = sem("o_lo")
        projected = sem("projected")
        added = sem("added")
        normed = sem("normed")
        guessed = sem("guessed")
        x1_done = sem("x1_done")
        scaled = sem("scaled")
        x1_turned = sem("x1_turned")
        x1T_done = sem("x1T_done")
        routed = sem("routed")
        logits_done = sem("logits_done")
        x1_stored = [sem(f"x1_stored{i}") for i in range(2)]

        def heads(slot, g):
            return o_in[:, slot, g].rearrange("p (a n) -> p a n", n=OROW)[:, :, 0:2 * HD].rearrange(
                "p a (h d) -> p a h d", h=2)

        def stat(slot, which):
            return o_in[:, slot].rearrange("p g (a n) -> p g a n", n=OROW)[:, :, :, 2 * HD + which:2 * HD + which + 3:2]

        def spread(w):
            return w.rearrange("p (a h) -> p a h", h=2).unsqueeze(3).to_broadcast([P, PAIRS, 2, HD])

        with nc.Block() as block:
            @block.sync
            def _(sp):
                sp.dma_start(gain_sb[:], row_broadcast(gain)).then_inc(const_loaded, 16)
                sp.dma_start(shift_sb[:], row_broadcast(shift)).then_inc(const_loaded, 16)
                sp.dma_start(br[:, 0:N_GROUPS], row_broadcast(b_rg)).then_inc(const_loaded, 16)
                sp.dma_start(br[:, N_GROUPS:], row_broadcast(b_re)).then_inc(const_loaded, 16)
                sp.wait_ge(padded, 1)
                sp.dma_start(wr[:, :, 0:N_GROUPS], w_rg.rearrange("(k p) n -> p k n", p=P)).then_inc(const_loaded, 16)
                sp.dma_start(wr[:, :, N_GROUPS:N_LOGITS], w_re.rearrange("(k p) n -> p k n", p=P)
                             ).then_inc(const_loaded, 16)
                for k in range(KC):
                    if k >= 2:
                        sp.wait_ge(wo_lo_done, k - 1)
                    sp.dma_start(w_raw[:, k % 2, :], w_o[bass.ts(k, P), :]).then_inc(w_loaded[k % 2], 16)

                def load(t, u):
                    sp.wait_ge(merges, t + 1)
                    sp.dma_start(o_in[:, u], scratch.o[0:n_g, bass.ts(t, P), :].rearrange("g p n -> p g n")
                                 ).then_inc(o_loaded[u], 16)
                    sp.wait_ge(added, 2 * t + 2)
                    sp.dma_start(x_in[:, u], x[bass.ts(t, P), :]).then_inc(x_loaded[u], 16)

                staged(sp, TILES, [(0, load)])

            @block.tensor
            def _(pe):
                pe.sem_inc(projected, 4)
                pe.sem_inc(x1_turned, 4)
                pe.sem_inc(routed, 1)
                pe.wait_ge(const_loaded, 96)

                def turn_x(t, u):
                    pe.wait_ge(x1_done, t + 1)
                    for h in range(2):
                        pe.wait_ge(x1T_done, 2 * t + h + 1)
                        for k in range(4):
                            done = pe.transpose(ps_x[:, h, k, :], x1[:, u, bass.ts(4 * h + k, P)], ident[:])
                        done.then_inc(x1_turned, 1)

                def turn_o(t, u):
                    pe.wait_ge(merges, t + 3)
                    for h in range(2):
                        pe.wait_ge(o_lo, 2 * t + h + 1)
                        for k in range(4):
                            done = pe.transpose(ps_o[:, h, k, :], merged[:, bass.ts(4 * h + k, P)], ident[:])
                        done.then_inc(o_turned, 1)

                def project(t, u):
                    pe.wait_ge(o_lo, 2 * t + 4)
                    pe.wait_ge(wo_lo_done, KC)
                    for h in range(2):
                        pe.wait_ge(added, 2 * t + h + 3)
                        for k in range(KC):
                            cols = bass.ts(h, HALF)
                            parts = ((oT_hi[:, u, k], wo_hi[:, k, cols]), (oT_hi[:, u, k], wo_lo[:, k, cols]),
                                     (oT_lo[:, u, k], wo_hi[:, k, cols]))
                            for m, (stationary, moving) in enumerate(parts):
                                done = pe.matmul(ps_h[:, h, :], stationary, moving, start=(k == 0 and m == 0),
                                                 stop=(k == KC - 1 and m == 2))
                        done.then_inc(projected, 1)

                def route(t, u):
                    pe.wait_ge(x1T_done, 2 * t + 4)
                    pe.wait_ge(logits_done, t + 1)
                    for k in range(KC):
                        done = pe.matmul(ps_l[:], x1T[:, k, :], wr[:, k, :], start=(k == 0), stop=(k == KC - 1))
                    done.then_inc(routed, 1)

                staged(pe, TILES, [(2, turn_x), (0, turn_o), (0, project), (2, route)])

            @block.scalar
            def _(act):
                act.sem_inc(x1T_done, 2)
                for i in range(2):
                    act.sem_inc(x1_stored[i], 16)
                for k in range(KC):
                    act.wait_ge(w_loaded[k % 2], 16 * (k // 2 + 1))
                    act.activation(wo_hi[:, k, :], w_raw[:, k % 2, :], ACT.Copy).then_inc(wo_hi_done, 1)

                def exp(t, u):
                    if n_g > 1:
                        act.wait_ge(mix, MIX * t + 2)
                        act.activation(part[:], gap[:], ACT.Exp).then_inc(exped, 1)

                def store(t, u):
                    act.wait_ge(x1_done, t + 1)
                    act.dma_start(scratch.x1[bass.ts(t, P), :], x1[:, u, :]).then_inc(x1_stored[u], 16)

                def copy_x(t, u):
                    for h in range(2):
                        act.wait_ge(x1_turned, 2 * t + h + 5)
                        act.wait_ge(routed, t + 1)
                        act.activation(x1T[:, 4 * h:4 * h + 4, :], ps_x[:, h], ACT.Copy).then_inc(x1T_done, 1)

                def hi(t, u):
                    for h in range(2):
                        act.wait_ge(o_turned, 2 * t + h + 1)
                        act.wait_ge(projected, 2 * t + 2)
                        act.activation(oT_hi[:, u, 4 * h:4 * h + 4, :], ps_o[:, h], ACT.Copy).then_inc(o_hi, 1)

                staged(act, TILES, [(0, exp), (2, store), (2, copy_x), (0, hi)])
                for i in range(2):
                    act.wait_ge(x1_stored[i], 16 * (TILES // 2 + 1))

            @block.gpsimd
            def _(pool):
                pool.memset(power[:], -0.5).then_inc(scaled, 1)
                pool.wait_ge(scaled, 1)
                pool.wait_ge(const_loaded, 96)

                def weigh_middle(t, u):
                    if n_g > 1:
                        pool.wait_ge(mix, MIX * t + 5)
                        pool.tensor_tensor(heads(u, 1), heads(u, 1), spread(weight[:, 1, :]), ALU.mult
                                           ).then_inc(middle, 1)

                def guess_root(t, u):
                    pool.wait_ge(normed, NORM * t + 4)
                    pool.tensor_tensor(guess[:, u], mean_var[:, u, 1:2], power[:], ALU.pow).then_inc(guessed, 1)

                def affine(t, u):
                    pool.wait_ge(normed, NORM * t + 8)
                    pool.tensor_tensor(x1[:, u], x1[:, u], gain_sb[:], ALU.mult).then_inc(scaled, 1)
                    pool.wait_ge(scaled, t + 2)
                    pool.tensor_tensor(x1[:, u], x1[:, u], shift_sb[:], ALU.add).then_inc(x1_done, 1)

                staged(pool, TILES, [(0, weigh_middle), (1, guess_root), (1, affine)])

            @block.vector
            def _(dve):
                dve.sem_inc(merges, 2)
                dve.sem_inc(o_lo, 2)
                dve.sem_inc(added, 4)
                dve.sem_inc(logits_done, 1)
                dve.memset(wr[:], 0.0).then_inc(padded, 1)
                dve.wait_ge(const_loaded, 96)
                for k in range(KC):
                    dve.wait_ge(wo_hi_done, k + 1)
                    dve.tensor_tensor(wo_lo[:, k, :], w_raw[:, k % 2, :], wo_hi[:, k, :].bitcast(F32), ALU.subtract
                                      ).then_inc(wo_lo_done, 1)

                def mix_branches(t, u):
                    dve.wait_ge(o_loaded[u], 16 * rounds(t, u))
                    dense = merged[:].rearrange("p (a h d) -> p a h d", a=PAIRS, h=2)
                    if n_g == 1:
                        dve.reciprocal(weight[:, 0, :].rearrange("p (a h) -> p a h", h=2), stat(u, 1)[:, 0]
                                       ).then_inc(mix, 1)
                        dve.wait_ge(mix, t + 1)
                        if not first(t):
                            dve.wait_ge(o_turned, 2 * t)
                        dve.tensor_tensor(dense, heads(u, 0), spread(weight[:, 0, :]), ALU.mult).then_inc(merges, 1)
                        return
                    base = MIX * t
                    dve.tensor_reduce(low[:].rearrange("p (a h) -> p a h", h=2),
                                      stat(u, 0).rearrange("p g a h -> p a h g"), AX.X, ALU.min).then_inc(mix, 1)
                    dve.wait_ge(mix, base + 1)
                    dve.tensor_tensor(gap[:].rearrange("p g (a h) -> p g a h", h=2),
                                      low[:].rearrange("p (a h) -> p a h", h=2).unsqueeze(1).to_broadcast(
                                          [P, n_g, PAIRS, 2]), stat(u, 0), ALU.subtract).then_inc(mix, 1)
                    dve.wait_ge(exped, t + 1)
                    dve.tensor_tensor(mass[:].rearrange("p g (a h) -> p g a h", h=2),
                                      part[:].rearrange("p g (a h) -> p g a h", h=2), stat(u, 1), ALU.mult
                                      ).then_inc(mix, 1)
                    dve.wait_ge(mix, base + 3)
                    dve.tensor_reduce(total[:], mass[:].rearrange("p g h -> p h g"), AX.X, ALU.add).then_inc(mix, 1)
                    dve.wait_ge(mix, base + 4)
                    dve.reciprocal(inverse[:], total[:]).then_inc(small, 1)
                    dve.wait_ge(small, 3 * t + 1)
                    dve.tensor_tensor(weight[:], part[:], inverse[:].unsqueeze(1).to_broadcast([P, n_g, HEADS]),
                                      ALU.mult).then_inc(mix, 1)
                    dve.wait_ge(mix, base + 5)
                    dve.tensor_tensor(heads(u, 0), heads(u, 0), spread(weight[:, 0, :]), ALU.mult)\
                       .then_inc(small, 1)
                    dve.tensor_tensor(heads(u, 2), heads(u, 2), spread(weight[:, 2, :]), ALU.mult)\
                       .then_inc(small, 1)
                    dve.wait_ge(small, 3 * t + 3)
                    if not first(t):
                        dve.wait_ge(o_turned, 2 * t)
                    dve.tensor_tensor(dense, heads(u, 0), heads(u, 2), ALU.add).then_inc(outer, 1)
                    dve.wait_ge(outer, t + 1)
                    dve.wait_ge(middle, t + 1)
                    dve.tensor_tensor(dense, dense, heads(u, 1), ALU.add).then_inc(merges, 1)

                def add_residual(t, u):
                    dve.wait_ge(x_loaded[u], 16 * rounds(t, u))
                    if not first(t):
                        dve.wait_ge(normed, NORM * t)
                    for h in range(2):
                        dve.wait_ge(projected, 2 * t + h + 5)
                        dve.scalar_tensor_tensor(out=res[:, bass.ts(h, HALF)], in0=x_in[:, u, bass.ts(h, HALF)],
                                                 scalar=ALPHA, in1=ps_h[:, h, :], op0=ALU.mult, op1=ALU.add
                                                 ).then_inc(added, 1)

                def lo(t, u):
                    for h in range(2):
                        dve.wait_ge(o_hi, 2 * t + h + 1)
                        at = (slice(None), u, slice(4 * h, 4 * h + 4))
                        dve.tensor_tensor(oT_lo[at], ps_o[:, h], oT_hi[at].bitcast(F32), ALU.subtract
                                          ).then_inc(o_lo, 1)

                def norm(t, u):
                    base = NORM * t
                    for h in range(2):
                        dve.wait_ge(added, 2 * t + h + 5)
                        dve.bn_stats(stats[:, h, :], res[:, bass.ts(h, HALF)]).then_inc(normed, 1)
                    dve.wait_ge(normed, base + 2)
                    dve.sem_inc(stepped, 1)
                    dve.bn_aggr(mean_var[:, u, :], stats[:]).then_inc(normed, 1)
                    dve.wait_ge(normed, base + 3)
                    dve.tensor_scalar(mean_var[:, u, 1:2], mean_var[:, u, 1:2], LN_EPS, None, ALU.add
                                      ).then_inc(normed, 1)
                    dve.wait_ge(guessed, t + 1)
                    dve.scalar_tensor_tensor(out=check[:], in0=mean_var[:, u, 1:2], scalar=guess[:, u],
                                             in1=guess[:, u], op0=ALU.mult, op1=ALU.mult).then_inc(normed, 1)
                    dve.wait_ge(normed, base + 5)
                    dve.tensor_scalar(fix[:], check[:], -0.5, 1.5, ALU.mult, ALU.add).then_inc(normed, 1)
                    dve.wait_ge(normed, base + 6)
                    dve.tensor_tensor(rstd[:], guess[:, u], fix[:], ALU.mult).then_inc(normed, 1)
                    dve.wait_ge(normed, base + 7)
                    dve.wait_ge(x1_stored[u], 16 * rounds(t, u))
                    dve.wait_ge(x1_turned, 2 * t + 2)
                    dve.tensor_scalar(x1[:, u], res[:], mean_var[:, u, 0:1], rstd[:], ALU.subtract, ALU.mult
                                      ).then_inc(normed, 1)

                def keep_logits(t, u):
                    dve.wait_ge(routed, t + 2)
                    at = logits[:, t] if isinstance(t, int) else logits[:, bass.ds(t, 1)].rearrange("p a n -> p (a n)")
                    dve.tensor_tensor(at, ps_l[:, 0:N_LOGITS], br[:], ALU.add).then_inc(logits_done, 1)

                staged(dve, TILES, [(0, mix_branches), (1, add_residual), (0, lo), (1, norm), (3, keep_logits)])


class Routing:

    def __init__(self, ctx, nc, tag):
        def sb(name, shape, dt=F32):
            return ctx.enter_context(nc.sbuf_tensor(f"{tag}_{name}", shape, dt))

        self.logits = sb("logits", [P, TILES, N_GROUPS + N_EXPERTS])
        self.gates = sb("gates", [P, TILES, TOP_K])
        self.slots = sb("slots", [P, TILES, TOP_K], U32)
        self.table = sb("table", [1, 5, BLOCKS + 1], I32)
        self.EXPERT, self.NEW, self.COUNT, self.USED, self.TOTAL = range(5)


def route_tokens(nc, tag, routing, c_iota, c_before, scratch):
    with ExitStack() as ctx:
        def sb(name, shape, dt=F32):
            return ctx.enter_context(nc.sbuf_tensor(f"{tag}_{name}", shape, dt))

        sem = ctx.enter_context(phase_semaphores(nc, tag))

        T, G, E, B = TILES, N_GROUPS, N_EXPERTS, BLOCKS + 1
        RING = 4
        iota = sb("iota", [P, B])
        before = sb("before", [P, P])
        ones = sb("ones", [P, P])
        rows = sb("rows", [P, RING, D])
        one = {n: sb(n, [P, T]) for n in ("g_max", "g_sum", "g_prob", "g_at", "max1", "at1", "max2", "at2", "gap",
                                          "gap_exp", "both", "share", "slot1", "slot2")}
        g_shift, g_exp, g_rank, g_one = (sb(n, [P, T, G]) for n in ("g_shift", "g_exp", "g_rank", "g_one"))
        masked, rank, one1, one2, both, base, picked = (sb(n, [P, T, E]) for n in (
            "masked", "rank", "one1", "one2", "chosen", "base", "picked"))
        totals, resets, running = (sb(n, [P, E, T]) for n in ("totals", "resets", "running"))
        steps = sb("steps", [P, MAX_BLOCKS_OF_ONE])
        over = sb("over", [P, E, MAX_BLOCKS_OF_ONE])
        n_blocks, ends, starts = (sb(n, [P, E]) for n in ("n_blocks", "ends", "starts"))
        passed = sb("passed", [1, B, E])
        expert, change, used, new, count = (sb(n, [1, B]) for n in ("expert", "change", "used", "new", "count"))
        ps_before = ctx.enter_context(nc.psum_tensor(f"{tag}_ps_before", [P, T, E], F32))
        ps_total = ctx.enter_context(nc.psum_tensor(f"{tag}_ps_total", [P, T, E], F32))

        const_loaded = sem("const_loaded")
        chain = sem("chain")
        shifted = sem("shifted")
        exped = sem("exped")
        chosen = sem("chosen")
        counted = sem("counted")
        placed = sem("placed")
        rows_loaded = [sem(f"rows_loaded{i}") for i in range(RING)]
        scattered = [sem(f"scattered{i}") for i in range(RING)]

        logits, gates = routing.logits, routing.gates
        g_log = logits[:, :, 0:G]
        e_log = logits[:, :, G:G + E]

        def wide(x, n):
            return x.unsqueeze(2).to_broadcast([P, T, n])

        def over_tiles(row):
            return row.unsqueeze(1).to_broadcast([P, T, row.shape[-1]])

        with nc.Block() as block:
            @block.sync
            def _(sp):
                sp.dma_start(iota[:], c_iota).then_inc(const_loaded, 16)
                sp.dma_start(before[:], c_before).then_inc(const_loaded, 16)
                for t in range(TILES):
                    if t >= RING:
                        sp.wait_ge(scattered[t % RING], 16 * TOP_K * (t // RING))
                    sp.dma_start(rows[:, t % RING, :], scratch.x1[bass.ts(t, P), :]
                                 ).then_inc(rows_loaded[t % RING], 16)

            @block.gpsimd
            def _(pool):
                pool.wait_ge(placed, 1)
                for t in range(TILES):
                    pool.wait_ge(rows_loaded[t % RING], 16 * (t // RING + 1))
                    for k in range(TOP_K):
                        pool.indirect_dma_start(
                            out=scratch.xs, out_offset=bass.IndirectOffsetOnAxis(
                                ap=routing.slots[:, t, k:k + 1], axis=0),
                            in_=rows[:, t % RING, :], in_offset=None).then_inc(scattered[t % RING], 16)
                for i in range(RING):
                    pool.wait_ge(scattered[i], 16 * TOP_K * (TILES // RING))

            @block.tensor
            def _(pe):
                pe.wait_ge(const_loaded, 32)
                pe.wait_ge(chosen, 2)
                every = both[:].rearrange("p t e -> p (t e)")
                pe.matmul(ps_before[:].rearrange("p t e -> p (t e)"), before[:], every, start=True, stop=True)
                pe.matmul(ps_total[:].rearrange("p t e -> p (t e)"), ones[:], every, start=True, stop=True
                          ).then_inc(counted, 1)

            @block.scalar
            def _(act):
                act.wait_ge(shifted, 1)
                act.activation(g_exp[:], g_shift[:], ACT.Exp).then_inc(exped, 1)
                act.wait_ge(shifted, 2)
                act.activation(one["gap_exp"][:], one["gap"][:], ACT.Exp).then_inc(exped, 1)

            @block.vector
            def _(dve):
                steps_done = [0]

                def link(ins):
                    steps_done[0] += 1
                    ins.then_inc(chain, 1)
                    dve.wait_ge(chain, steps_done[0])

                def tt(out, a, b, op):
                    link(dve.tensor_tensor(out, a, b, op))

                def first_of_max(values, maximum, at, n, ranks, ones_out):
                    link(dve.tensor_reduce(maximum, values, AX.X, ALU.max))
                    tt(ranks, values, wide(maximum, n), ALU.is_lt)
                    link(dve.scalar_tensor_tensor(out=ranks, in0=ranks, scalar=1000.0, in1=over_tiles(iota[:, 0:n]),
                                                  op0=ALU.mult, op1=ALU.add))
                    link(dve.tensor_reduce(at, ranks, AX.X, ALU.min))
                    tt(ones_out, over_tiles(iota[:, 0:n]), wide(at, n), ALU.is_equal)

                o = {k: v[:] for k, v in one.items()}
                dve.memset(ones[:], 1.0).then_inc(chosen, 1)
                link(dve.memset(routing.table[:], 0))
                link(dve.memset(resets[:], 1.0))
                link(dve.memset(resets[:, :, 0:1], 0.0))
                dve.wait_ge(const_loaded, 32)
                first_of_max(g_log, o["g_max"], o["g_at"], G, g_rank[:], g_one[:])
                dve.tensor_tensor(g_shift[:], g_log, wide(o["g_max"], G), ALU.subtract).then_inc(shifted, 1)
                link(dve.tensor_scalar(g_rank[:], g_one[:], -1.0, -NEG, ALU.add, ALU.mult))
                tt(masked[:].rearrange("p t (g n) -> p t g n", g=G), e_log.rearrange("p t (g n) -> p t g n", g=G),
                   g_rank[:].unsqueeze(3).to_broadcast([P, T, G, PER_GROUP]), ALU.add)
                first_of_max(masked[:], o["max1"], o["at1"], E, rank[:], one1[:])
                link(dve.scalar_tensor_tensor(out=masked[:], in0=one1[:], scalar=2 * NEG, in1=masked[:],
                                              op0=ALU.mult, op1=ALU.add))
                first_of_max(masked[:], o["max2"], o["at2"], E, rank[:], one2[:])
                dve.tensor_tensor(both[:], one1[:], one2[:], ALU.add).then_inc(chosen, 1)
                dve.tensor_tensor(o["gap"], o["max2"], o["max1"], ALU.subtract).then_inc(shifted, 1)
                dve.wait_ge(exped, 1)
                link(dve.tensor_reduce(o["g_sum"], g_exp[:], AX.X, ALU.add))
                link(dve.reciprocal(o["g_prob"], o["g_sum"]))
                dve.wait_ge(exped, 2)
                link(dve.tensor_scalar(o["both"], o["gap_exp"], 1.0, None, ALU.add))
                link(dve.reciprocal(o["share"], o["both"]))
                tt(gates[:, :, 0], o["share"], o["g_prob"], ALU.mult)
                tt(gates[:, :, 1], gates[:, :, 0], o["gap_exp"], ALU.mult)
                dve.wait_ge(counted, 1)
                link(dve.tensor_copy(totals[:], ps_total[:].rearrange("p t e -> p e t")))
                flat = [x[:].rearrange("p e t -> p (e t)") for x in (running, resets, totals)]
                link(dve.tensor_tensor_scan(flat[0], flat[1], flat[2], 0.0, ALU.mult, ALU.add))
                link(dve.tensor_scalar(steps[:], iota[:, 0:MAX_BLOCKS_OF_ONE], float(P), None, ALU.mult))
                tt(over[:], running[:, :, T - 1:T].to_broadcast([P, E, MAX_BLOCKS_OF_ONE]),
                   steps[:].unsqueeze(1).to_broadcast([P, E, MAX_BLOCKS_OF_ONE]), ALU.is_gt)
                link(dve.tensor_reduce(n_blocks[:], over[:], AX.X, ALU.add))
                link(dve.tensor_tensor_scan(ends[:], ones[:, 0:E], n_blocks[:], 0.0, ALU.mult, ALU.add))
                tt(starts[:], ends[:], n_blocks[:], ALU.subtract)
                link(dve.tensor_scalar(starts[:], starts[:], float(P), None, ALU.mult))
                tt(running[:], running[:], totals[:], ALU.subtract)
                tt(base[:], running[:].rearrange("p e t -> p t e"), over_tiles(starts[:]), ALU.add)
                tt(base[:], ps_before[:], base[:], ALU.add)
                for which, slot, k in ((one1, "slot1", 0), (one2, "slot2", 1)):
                    tt(picked[:], which[:], base[:], ALU.mult)
                    link(dve.tensor_reduce(o[slot], picked[:], AX.X, ALU.add))
                    link(dve.tensor_copy(routing.slots[:, :, k], o[slot]))
                dve.sem_inc(placed, 1)
                tt(passed[:], iota[0:1, :].unsqueeze(2).to_broadcast([1, B, E]),
                   ends[0:1, :].unsqueeze(1).to_broadcast([1, B, E]), ALU.is_ge)
                link(dve.tensor_reduce(expert[:], passed[:], AX.X, ALU.add))
                tt(used[:], iota[0:1, :], ends[0:1, E - 1:E].to_broadcast([1, B]), ALU.is_lt)
                link(dve.memset(change[:, 0:1], 1.0))
                tt(change[:, 1:B], expert[:, 1:B], expert[:, 0:B - 1], ALU.is_gt)
                tt(new[:], change[:], used[:], ALU.mult)
                link(dve.tensor_tensor_scan(count[:], ones[0:1, 0:B], new[:], 0.0, ALU.mult, ALU.add))
                link(dve.tensor_scalar(expert[:], expert[:], float(E - 1), None, ALU.min))
                for row, values in ((routing.EXPERT, expert), (routing.NEW, new), (routing.COUNT, count),
                                    (routing.USED, used)):
                    link(dve.tensor_copy(routing.table[:, row, :], values[:]))
                link(dve.tensor_copy(routing.table[:, routing.TOTAL, 0:1], ends[0:1, E - 1:E]))


def experts(nc, tag, routing, w1, w3, w2, ident, scratch):
    with ExitStack() as ctx:
        def sb(name, shape, dt=F32):
            return ctx.enter_context(nc.sbuf_tensor(f"{tag}_{name}", shape, dt))

        def ps(name, shape):
            return ctx.enter_context(nc.psum_tensor(f"{tag}_{name}", shape, F32))

        sem = ctx.enter_context(phase_semaphores(nc, tag))

        FC = D_EXPERT // P
        LOADS = EXPERT_PIECES // 2
        w_raw = sb("w_raw", [P, EXPERT_PIECES, D])
        w_hi = sb("w_hi", [P, EXPERT_PIECES, D], F32R)
        w_lo = sb("w_lo", [P, EXPERT_PIECES, D], F32R)
        x_row = sb("x_row", [P, D])
        xT_hi = sb("xT_hi", [P, KC, P], F32R)
        xT_lo = sb("xT_lo", [P, KC, P], F32R)
        gate = sb("gate", [P, D_EXPERT])
        hidden = sb("hidden", [P, D_EXPERT])
        hT_hi = sb("hT_hi", [P, FC, P], F32R)
        hT_lo = sb("hT_lo", [P, FC, P], F32R)
        y = sb("y", [P, D])
        ps_x = ps("ps_x", [P, 2, 4, P])
        ps_gate = ps("ps_gate", [P, D_EXPERT])
        ps_up = ps("ps_up", [P, D_EXPERT])
        ps_h = ps("ps_h", [P, FC, P])
        ps_y = ps("ps_y", [P, 2, HALF])

        w_loaded = [sem(f"w_loaded{i}") for i in range(LOADS)]
        x_loaded = sem("x_loaded")
        x_turned = sem("x_turned")
        x_hi = sem("x_hi")
        x_lo = sem("x_lo")
        w13_hi = sem("w13_hi")
        w13_lo = sem("w13_lo")
        w13_used = sem("w13_used")
        w2_hi = sem("w2_hi")
        w2_lo = sem("w2_lo")
        w2_used = sem("w2_used")
        gated = sem("gated")
        hidden_done = sem("hidden_done")
        h_turned = sem("h_turned")
        h_hi = sem("h_hi")
        h_lo = sem("h_lo")
        y_done = sem("y_done")
        y_stored = sem("y_stored")
        all_stored = sem("all_stored")
        table = routing.table

        def entry(eng, row, b, most):
            at = table[0:1, row, b:b + 1] if isinstance(b, int) else table[0:1, row, bass.ds(b, 1)]
            return eng.value_load(at, min_val=0, max_val=most)

        def over_blocks(eng, body):
            with eng.Fori(1, BLOCKS) as b:
                used = entry(eng, routing.USED, b, 1)
                with eng.If(used > 0):
                    body(b)

        def used_blocks(eng):
            return eng.value_load(table[0:1, routing.TOTAL, 0:1], min_val=1, max_val=BLOCKS)

        with nc.Block() as block:
            @block.sync
            def _(sp):
                def load_x(b):
                    sp.wait_ge(x_turned, 2 * b + 2)
                    sp.dma_start(x_row[:], scratch.xs[bass.ds(b * P, P), :]).then_inc(x_loaded, 16)

                def load_w(b):
                    e = entry(sp, routing.EXPERT, b, N_EXPERTS - 1)
                    n = entry(sp, routing.COUNT, b, N_EXPERTS)
                    for i in range(LOADS):
                        if i < LOADS - 2:
                            sp.wait_ge(w13_lo, W13_PIECES * n + 2 * i + 2)
                            w = (w1, w3)[i // 2][bass.ds(e, 1), (i % 2) * HALF:(i % 2 + 1) * HALF, :]
                            src = w.rearrange("a (k p) f -> p (a k) f", p=P)
                            dst = w_raw[:, 2 * i:2 * i + 2, :].rearrange("p a (k f) -> p (a k) f", k=2)
                        else:
                            j = i - (LOADS - 2)
                            sp.wait_ge(w2_lo, W2_PIECES * n + 2 * j + 2)
                            src = w2[bass.ds(e, 1), 2 * j * P:2 * (j + 1) * P, :].rearrange(
                                "a (k p) n -> p (a k) n", p=P)
                            dst = w_raw[:, 2 * i:2 * i + 2, :]
                        sp.dma_start(dst, src).then_inc(w_loaded[i], 16)

                load_x(0)
                load_w(0)

                def loads(b):
                    load_x(b + 1)
                    with sp.If(entry(sp, routing.NEW, b + 1, 1) > 0):
                        load_w(b + 1)

                loads(0)
                over_blocks(sp, loads)

            @block.tensor
            def _(pe):
                pe.sem_inc(x_turned, 2)
                pe.sem_inc(w13_used, W13_PIECES)
                pe.sem_inc(w2_used, W2_PIECES)
                pe.sem_inc(h_turned, 1)

                def turn_x(b):
                    pe.wait_ge(x_loaded, 16 * b + 16)
                    for h in range(2):
                        if not first(b):
                            pe.wait_ge(x_lo, 2 * b + h - 1)
                        for k in range(4):
                            done = pe.transpose(ps_x[:, h, k, :], x_row[:, bass.ts(4 * h + k, P)], ident[:])
                        done.then_inc(x_turned, 1)

                def products(out, stationary, moving, k_first, k_last):
                    hi, lo = stationary
                    m_hi, m_lo = moving
                    pe.matmul(out, hi, m_hi, start=k_first, stop=False)
                    pe.matmul(out, hi, m_lo, start=False, stop=False)
                    return pe.matmul(out, lo, m_hi, start=False, stop=k_last)

                def up(b):
                    n = entry(pe, routing.COUNT, b, N_EXPERTS)
                    pe.wait_ge(x_lo, 2 * b + 2)
                    pe.wait_ge(hidden_done, b + 1)
                    for p in range(W13_PIECES):
                        pe.wait_ge(w13_lo, W13_PIECES * (n + 1) + p + 1)
                        out = (ps_gate, ps_up)[p // 4]
                        for j in range(2):
                            k = 2 * (p % 4) + j
                            cols = bass.ts(j, D_EXPERT)
                            done = products(out[:], (xT_hi[:, k, :], xT_lo[:, k, :]),
                                            (w_hi[:, p, cols], w_lo[:, p, cols]), k == 0, k == KC - 1)
                        done.then_inc(w13_used, 1)

                def down(b):
                    n = entry(pe, routing.COUNT, b, N_EXPERTS)
                    pe.wait_ge(h_lo, b + 1)
                    pe.wait_ge(y_done, 2 * b + 2)
                    for k in range(FC):
                        pe.wait_ge(w2_lo, W2_PIECES * (n + 1) + k + 1)
                        p = W13_PIECES + k
                        for h in range(2):
                            cols = bass.ts(h, HALF)
                            done = products(ps_y[:, h, :], (hT_hi[:, k, :], hT_lo[:, k, :]),
                                            (w_hi[:, p, cols], w_lo[:, p, cols]), k == 0, k == FC - 1)
                        done.then_inc(w2_used, 1)

                def turn_h(b):
                    pe.wait_ge(hidden_done, b + 2)
                    if not first(b):
                        pe.wait_ge(h_lo, b)
                    for k in range(FC):
                        done = pe.transpose(ps_h[:, k, :], hidden[:, bass.ts(k, P)], ident[:])
                    done.then_inc(h_turned, 1)

                turn_x(0)
                up(0)
                turn_x(1)
                turn_h(0)

                def body(b):
                    up(b)
                    turn_x(b + 1)
                    down(b - 1)
                    turn_h(b)

                over_blocks(pe, body)
                down(used_blocks(pe) - 1)

            def split_w13(eng, b, pieces, part):
                n = entry(eng, routing.COUNT, b, N_EXPERTS)
                for p in pieces:
                    if part == "hi":
                        if p % 2 == 0:
                            eng.wait_ge(w_loaded[p // 2], 16 * n)
                        eng.wait_ge(w13_used, W13_PIECES * b + p + 1)
                        eng.activation(w_hi[:, p, :], w_raw[:, p, :], ACT.Copy).then_inc(w13_hi, 1)
                    else:
                        eng.wait_ge(w13_hi, W13_PIECES * n + p + 1)
                        eng.tensor_tensor(w_lo[:, p, :], w_raw[:, p, :], w_hi[:, p, :].bitcast(F32), ALU.subtract
                                          ).then_inc(w13_lo, 1)

            @block.scalar
            def _(act):
                act.sem_inc(y_done, 2)
                act.sem_inc(w13_hi, W13_PIECES)
                act.sem_inc(w2_hi, W2_PIECES)
                act.sem_inc(y_stored, 16)

                def if_new(b, body):
                    if first(b):
                        body()
                        return
                    with act.If(entry(act, routing.NEW, b, 1) > 0):
                        body()

                def silu(b):
                    act.wait_ge(w13_used, W13_PIECES * b + W13_PIECES + 4)
                    act.wait_ge(hidden_done, b + 1)
                    act.activation(gate[:], ps_gate[:], ACT.Silu).then_inc(gated, 1)

                def x_parts(b):
                    for h in range(2):
                        act.wait_ge(x_turned, 2 * b + h + 3)
                        act.wait_ge(w13_used, W13_PIECES * b + W13_PIECES)
                        act.activation(xT_hi[:, 4 * h:4 * h + 4, :], ps_x[:, h], ACT.Copy).then_inc(x_hi, 1)

                def split_w2(b):
                    n = entry(act, routing.COUNT, b, N_EXPERTS)
                    for k in range(W2_PIECES):
                        if k % 2 == 0:
                            act.wait_ge(w_loaded[4 + k // 2], 16 * n)
                        act.wait_ge(w2_used, W2_PIECES * b + k + 1)
                        p = W13_PIECES + k
                        act.activation(w_hi[:, p, :], w_raw[:, p, :], ACT.Copy).then_inc(w2_hi, 1)

                def outputs(b):
                    act.wait_ge(y_stored, 16 * b + 16)
                    act.wait_ge(w2_used, W2_PIECES * b + 2 * W2_PIECES)
                    for h in range(2):
                        act.activation(y[:, bass.ts(h, HALF)], ps_y[:, h, :], ACT.Copy).then_inc(y_done, 1)
                    act.wait_ge(y_done, 2 * b + 4)
                    act.dma_start(scratch.ys[bass.ds(b * P, P), :], y[:]).then_inc(y_stored, 16)

                def h_parts(b):
                    act.wait_ge(h_turned, b + 2)
                    act.wait_ge(w2_used, W2_PIECES * b + W2_PIECES)
                    act.activation(hT_hi[:], ps_h[:], ACT.Copy).then_inc(h_hi, 1)

                split_w13(act, 0, range(W13_PIECES), "hi")
                x_parts(0)
                silu(0)

                def rest(b, before):
                    if_new(b + 1, lambda: split_w13(act, b + 1, range(4, 8), "hi"))
                    x_parts(b + 1)
                    if_new(b, lambda: split_w2(b))
                    if before:
                        outputs(b - 1)
                    h_parts(b)

                if_new(1, lambda: split_w13(act, 1, range(4), "hi"))
                rest(0, False)

                def body(b):
                    if_new(b + 1, lambda: split_w13(act, b + 1, range(4), "hi"))
                    silu(b)
                    rest(b, True)

                over_blocks(act, body)
                total = used_blocks(act)
                outputs(total - 1)
                act.wait_ge(y_stored, 16 * total + 16)
                act.sem_inc(all_stored, 1)

            @block.vector
            def _(dve):
                dve.sem_inc(w13_lo, 2 * W13_PIECES)
                dve.sem_inc(hidden_done, 1)

                def if_new(b, body):
                    with dve.If(entry(dve, routing.NEW, b, 1) > 0):
                        body()

                def multiply(b):
                    dve.wait_ge(gated, b + 1)
                    dve.wait_ge(w13_used, W13_PIECES * b + 2 * W13_PIECES)
                    dve.wait_ge(h_turned, b + 1)
                    dve.tensor_tensor(hidden[:], gate[:], ps_up[:], ALU.mult).then_inc(hidden_done, 1)

                def x_parts(b):
                    for h in range(2):
                        dve.wait_ge(x_hi, 2 * b + h + 1)
                        at = (slice(None), slice(4 * h, 4 * h + 4))
                        dve.tensor_tensor(xT_lo[at], ps_x[:, h], xT_hi[at].bitcast(F32), ALU.subtract
                                          ).then_inc(x_lo, 1)

                def h_parts(b):
                    dve.wait_ge(h_hi, b + 1)
                    dve.tensor_tensor(hT_lo[:], ps_h[:], hT_hi[:].bitcast(F32), ALU.subtract).then_inc(h_lo, 1)

                split_w13(dve, 0, range(W13_PIECES), "lo")
                x_parts(0)

                def body(b):
                    if_new(b + 1, lambda: split_w13(dve, b + 1, range(W13_PIECES), "lo"))
                    multiply(b)
                    x_parts(b + 1)
                    h_parts(b)

                body(0)
                over_blocks(dve, body)

            @block.gpsimd
            def _(pool):
                pool.sem_inc(w2_lo, 2 * W2_PIECES)

                def split_w2(b):
                    n = entry(pool, routing.COUNT, b, N_EXPERTS)
                    for k in range(W2_PIECES):
                        p = W13_PIECES + k
                        pool.wait_ge(w2_hi, W2_PIECES * n + k + 1)
                        pool.tensor_tensor(w_lo[:, p, :], w_raw[:, p, :], w_hi[:, p, :].bitcast(F32), ALU.subtract
                                           ).then_inc(w2_lo, 1)

                split_w2(0)

                def body(b):
                    with pool.If(entry(pool, routing.NEW, b, 1) > 0):
                        split_w2(b)

                over_blocks(pool, body)


def sum_and_norm(nc, tag, routing, gain, shift, out, scratch):
    NORM = 8
    with ExitStack() as ctx:
        def sb(name, shape, dt=F32):
            return ctx.enter_context(nc.sbuf_tensor(f"{tag}_{name}", shape, dt))

        sem = ctx.enter_context(phase_semaphores(nc, tag))

        gain_sb = sb("gain", [P, D])
        shift_sb = sb("shift", [P, D])
        index = sb("index", [P, 2, TOP_K], U32)
        x1 = sb("x1", [P, 2, D])
        y_in = sb("y_in", [P, 2, TOP_K, D])
        res = sb("res", [P, D])
        stats = sb("stats", [P, 2, 6])
        mean_var = sb("mean_var", [P, 2, 2])
        power = sb("power", [P, 1])
        guess = sb("guess", [P, 2, 1])
        check, fix, rstd = (sb(n, [P, 1]) for n in ("check", "fix", "rstd"))
        x2 = sb("x2", [P, 2, D])

        const_loaded = sem("const_loaded")
        x1_loaded = [sem(f"x1_loaded{i}") for i in range(2)]
        gathered = [sem(f"gathered{i}") for i in range(2)]
        passed = sem("passed")
        indexed = sem("indexed")
        first_in = sem("first_in")
        second_in = sem("second_in")
        alphas = sem("alphas")
        normed = sem("normed")
        stepped = sem("stepped")
        guessed = sem("guessed")
        scaled = sem("scaled")
        done_rows = sem("done_rows")
        stored = [sem(f"stored{i}") for i in range(2)]

        with nc.Block() as block:
            @block.sync
            def _(sp):
                sp.dma_start(gain_sb[:], row_broadcast(gain)).then_inc(const_loaded, 16)
                sp.dma_start(shift_sb[:], row_broadcast(shift)).then_inc(const_loaded, 16)

                def load(t, u):
                    sp.wait_ge(second_in, t + 1)
                    sp.dma_start(x1[:, u, :], scratch.x1[bass.ts(t, P), :]).then_inc(x1_loaded[u], 16)

                staged(sp, TILES, [(0, load)])

            @block.gpsimd
            def _(pool):
                pool.memset(power[:], -0.5).then_inc(indexed, 1)
                pool.wait_ge(const_loaded, 32)

                def gather(t, u):
                    pool.wait_ge(second_in, t + 1)
                    slots = routing.slots[:, t, :] if isinstance(t, int) else \
                        routing.slots[:, bass.ds(t, 1), :].rearrange("p a n -> p (a n)")
                    pool.tensor_copy(index[:, u, :], slots).then_inc(indexed, 1)
                    pool.wait_ge(indexed, t + 2)
                    pool.sem_inc(passed, 1)
                    for k in range(TOP_K):
                        pool.indirect_dma_start(out=y_in[:, u, k, :], out_offset=None, in_=scratch.ys,
                                                in_offset=bass.IndirectOffsetOnAxis(ap=index[:, u, k:k + 1], axis=0)
                                                ).then_inc(gathered[u], 16)

                def guess_root(t, u):
                    pool.wait_ge(normed, NORM * t + 4)
                    pool.tensor_tensor(guess[:, u], mean_var[:, u, 1:2], power[:], ALU.pow).then_inc(guessed, 1)

                def affine(t, u):
                    pool.wait_ge(normed, NORM * t + 8)
                    pool.tensor_tensor(x2[:, u], x2[:, u], gain_sb[:], ALU.mult).then_inc(scaled, 1)
                    pool.wait_ge(scaled, t + 1)
                    pool.tensor_tensor(x2[:, u], x2[:, u], shift_sb[:], ALU.add).then_inc(done_rows, 1)

                staged(pool, TILES, [(0, gather), (1, guess_root), (1, affine)])

            @block.scalar
            def _(act):
                for i in range(2):
                    act.sem_inc(stored[i], 16)

                def scale(t, u):
                    act.wait_ge(x1_loaded[u], 16 * rounds(t, u))
                    act.activation(x1[:, u], x1[:, u], ACT.Copy, scale=ALPHA).then_inc(alphas, 1)

                def store(t, u):
                    act.wait_ge(done_rows, t + 1)
                    act.dma_start(out[bass.ts(t, P), :], x2[:, u, :]).then_inc(stored[u], 16)

                staged(act, TILES, [(0, scale), (2, store)])
                for i in range(2):
                    act.wait_ge(stored[i], 16 * (TILES // 2 + 1))

            @block.vector
            def _(dve):
                dve.sem_inc(second_in, 2)

                def gate(t, k):
                    if isinstance(t, int):
                        return routing.gates[:, t, k:k + 1]
                    return routing.gates[:, bass.ds(t, 1), k:k + 1].rearrange("p a n -> p (a n)")

                def add(t, u):
                    dve.wait_ge(alphas, t + 1)
                    dve.wait_ge(gathered[u], 16 * TOP_K * rounds(t, u))
                    dve.scalar_tensor_tensor(out=x1[:, u], in0=y_in[:, u, 0, :], scalar=gate(t, 0), in1=x1[:, u],
                                             op0=ALU.mult, op1=ALU.add).then_inc(first_in, 1)
                    dve.wait_ge(first_in, t + 1)
                    if not first(t):
                        dve.wait_ge(normed, NORM * t)
                    dve.scalar_tensor_tensor(out=res[:], in0=y_in[:, u, 1, :], scalar=gate(t, 1), in1=x1[:, u],
                                             op0=ALU.mult, op1=ALU.add).then_inc(second_in, 1)

                def norm(t, u):
                    base = NORM * t
                    dve.wait_ge(second_in, t + 3)
                    for h in range(2):
                        dve.bn_stats(stats[:, h, :], res[:, bass.ts(h, HALF)]).then_inc(normed, 1)
                    dve.wait_ge(normed, base + 2)
                    dve.sem_inc(stepped, 1)
                    dve.bn_aggr(mean_var[:, u, :], stats[:]).then_inc(normed, 1)
                    dve.wait_ge(normed, base + 3)
                    dve.tensor_scalar(mean_var[:, u, 1:2], mean_var[:, u, 1:2], LN_EPS, None, ALU.add
                                      ).then_inc(normed, 1)
                    dve.wait_ge(guessed, t + 1)
                    dve.scalar_tensor_tensor(out=check[:], in0=mean_var[:, u, 1:2], scalar=guess[:, u],
                                             in1=guess[:, u], op0=ALU.mult, op1=ALU.mult).then_inc(normed, 1)
                    dve.wait_ge(normed, base + 5)
                    dve.tensor_scalar(fix[:], check[:], -0.5, 1.5, ALU.mult, ALU.add).then_inc(normed, 1)
                    dve.wait_ge(normed, base + 6)
                    dve.tensor_tensor(rstd[:], guess[:, u], fix[:], ALU.mult).then_inc(normed, 1)
                    dve.wait_ge(normed, base + 7)
                    dve.wait_ge(stored[u], 16 * rounds(t, u))
                    dve.tensor_scalar(x2[:, u], res[:], mean_var[:, u, 0:1], rstd[:], ALU.subtract, ALU.mult
                                      ).then_inc(normed, 1)

                staged(dve, TILES, [(1, norm), (0, add)])


def grid_bias(nc, rpb, c_edge, c_inner, scratch):
    W = 2 * GRID_W - 1
    R_ROWS, R_COLS = 2 * NA_KH - 1, 2 * NA_KW - 1
    LEFT = GRID_W - 1 - (NA_KW - 1)
    HR = HEADS * R_ROWS
    with ExitStack() as ctx:
        def sb(name, shape, dt=F32):
            return ctx.enter_context(nc.sbuf_tensor(f"gb_{name}", shape, dt))

        sem = ctx.enter_context(phase_semaphores(nc, "gb"))
        wide = sb("wide", [HR // 2, 2, W])
        edge_mask = sb("edge_mask", [P, GRID_W])
        inner_mask = sb("inner_mask", [P, IN_TN, GRID_W])
        edge = sb("edge", [P, 2, NA_TN, GRID_W])
        inner = sb("inner", [P, 2, IN_TN, GRID_W])
        zeroed, const_loaded, widened, spread, masked = (
            sem(n) for n in ("zeroed", "const_loaded", "widened", "spread", "masked"))
        loaded = [sem(f"loaded{i}") for i in range(2)]
        stored = [sem(f"stored{i}") for i in range(2)]
        with nc.Block() as block:
            @block.sync
            def _(sp):
                sp.dma_start(edge_mask[:], c_edge).then_inc(const_loaded, 16)
                sp.dma_start(inner_mask[:].rearrange("p t c -> p (t c)"), c_inner).then_inc(const_loaded, 16)
                sp.wait_ge(zeroed, 1)
                rows = rpb.rearrange("h r c -> (h r) c").rearrange("(p u) c -> p u c", u=2)
                sp.dma_start(wide[:, :, LEFT:LEFT + R_COLS], rows).then_inc(widened, 16)
                sp.wait_ge(widened, 16)
                sp.dma_start(scratch.rpb_rows.rearrange("(p u) c -> p u c", u=2), wide[:]).then_inc(spread, 16)
                sp.wait_ge(spread, 16)
                for a in range(2):
                    for t in range(NA_TN):
                        src = bass.AP(scratch.rpb_rows.tensor, (t + NA_T0 - a + NA_KH - 1) * W + GRID_W - 1,
                                      [[R_ROWS * W, HEADS], [-1, GRID_W], [1, GRID_W]])
                        sp.dma_start(scratch.rpb_raw[:, bass.ts(a, GRID_W), bass.ts(t, GRID_W)], src).then_inc(spread, 16)
                sp.wait_ge(spread, 16 * (2 * NA_TN + 1))
                for h in range(HEADS):
                    if h >= 2:
                        sp.wait_ge(stored[h % 2], 32 * (h // 2))
                    sp.dma_start(edge[:, h % 2].rearrange("p t c -> p (t c)"), scratch.rpb_raw[h]
                                 ).then_inc(loaded[h % 2], 16)

            @block.vector
            def _(dve):
                dve.memset(wide[:], 0.0).then_inc(zeroed, 1)
                dve.wait_ge(const_loaded, 32)
                for h in range(HEADS):
                    dve.wait_ge(loaded[h % 2], 16 * (h // 2 + 1))
                    t0 = IN_T0 - NA_T0
                    dve.tensor_tensor(inner[:, h % 2], edge[:, h % 2, t0:t0 + IN_TN, :], inner_mask[:], ALU.add
                                      ).then_inc(masked, 1)
                    dve.wait_ge(masked, 2 * h + 1)
                    dve.tensor_tensor(edge[:, h % 2], edge[:, h % 2], edge_mask[:].unsqueeze(1).to_broadcast(
                        [P, NA_TN, GRID_W]), ALU.add).then_inc(masked, 1)

            @block.scalar
            def _(act):
                for h in range(HEADS):
                    act.wait_ge(masked, 2 * h + 2)
                    n = NA_TN * GRID_W
                    act.dma_start(scratch.bias_b[h, :, 0:n], edge[:, h % 2].rearrange("p t c -> p (t c)")
                                  ).then_inc(stored[h % 2], 16)
                    act.dma_start(scratch.bias_b[h, :, n:], inner[:, h % 2].rearrange("p t c -> p (t c)")
                                  ).then_inc(stored[h % 2], 16)
                for i in range(2):
                    act.wait_ge(stored[i], 32 * HEADS // 2)


def grid_attention(nc, ident, scratch):
    N_EDGE = NA_TN * GRID_W
    B_COLS_B = N_EDGE + IN_TN * GRID_W
    KMAX = 5
    jobs = []
    for i, (c0, n, moves, t0) in enumerate(grid_tiles()):
        col = (N_EDGE if moves else 0) + t0 * GRID_W
        for head in range(2):
            jobs.append((i, head, c0, n, col))
    JOBS = len(jobs)
    with ExitStack() as ctx:
        def sb(name, shape, dt=F32):
            return ctx.enter_context(nc.sbuf_tensor(f"ga_{name}", shape, dt))

        sem = ctx.enter_context(phase_semaphores(nc, "ga"))

        q_one = sb("q_one", [P, 2, 2, SEQ])
        k_two = sb("k_two", [P, 2, SEQ])
        v_two = sb("v_two", [P, 2, SEQ_TILES, P])
        bias = sb("bias", [P, 2, 2, B_COLS_B])
        minus_s = sb("minus_s", [P, 2, KMAX * P])
        prob = sb("prob", [P, 2, KMAX * P])
        probT = sb("probT", [P, 2, KMAX, P])
        rows = sb("rows", [P, 2, SEQ_TILES, OROW])
        ps_s = ctx.enter_context(nc.psum_tensor("ga_ps_s", [P, 2, 2, HALF], F32))
        ps_t = ctx.enter_context(nc.psum_tensor("ga_ps_t", [P, 2, 4, P], F32))
        ps_o = ctx.enter_context(nc.psum_tensor("ga_ps_o", [P, 2, 4, P], F32))

        zeroed = sem("zeroed")
        loaded = [sem(f"loaded{i}") for i in range(2)]
        scored = sem("scored")
        biased = sem("biased")
        stepped = sem("stepped")
        exped = sem("exped")
        turned = sem("turned")
        turned_sb = sem("turned_sb")
        summed = sem("summed")
        placed = sem("placed")
        stored = [sem(f"stored{i}") for i in range(2)]

        with nc.Block() as block:
            def loads(s, hp):
                ch = hp * P
                v = scratch.v[s, :, bass.ds(ch, P)].rearrange("(c p) n -> p c n", p=P)
                out = [(q_one[HD * head:HD * head + HD, s, head, :], scratch.qT[s, bass.ds(ch + HD * head, HD), :])
                       for head in range(2)]
                return out + [(k_two[:, s, :], scratch.kT[s, bass.ds(ch, P), :]), (v_two[:, s], v),
                              (bias[:, s], scratch.bias_b[bass.ds(2 * hp, 2)].rearrange("h p n -> p h n"))]

            N_LOAD = len(loads(0, 0))

            @block.sync
            def _(sp):
                sp.wait_ge(zeroed, 2)
                with sp.Fori(0, PAIRS) as hp:
                    for s in range(N_SEQ):
                        sp.wait_ge(summed, (2 * hp + s + 1) * JOBS)
                        for dst, src in loads(s, hp):
                            sp.dma_start(dst, src).then_inc(loaded[s], 16)

            @block.gpsimd
            def _(pool):
                pool.memset(q_one[0:HD, :, 1, :], 0.0).then_inc(zeroed, 1)
                pool.wait_ge(zeroed, 1)
                pool.memset(q_one[HD:P, :, 0, :], 0.0).then_inc(zeroed, 1)

            body = [(s, *job) for s in range(N_SEQ) for job in jobs]
            ALL = len(body)

            @block.tensor
            def _(pe):
                pe.sem_inc(turned, 4)
                pe.sem_inc(summed, 2 * JOBS)
                with pe.Fori(0, PAIRS) as hp:
                    base = hp * ALL

                    def scores(j):
                        s, i, head, c0, n, col = body[j]
                        if j % JOBS == 0:
                            pe.wait_ge(loaded[s], 16 * N_LOAD * (hp + 1))
                        pe.wait_ge(biased, base + j + 1)
                        done = pe.matmul(ps_s[:, j % 2, 0, :], q_one[:, s, head, bass.ts(i, P)],
                                         k_two[:, s, c0 * P:c0 * P + HALF], start=True, stop=True)
                        if n > 4:
                            done = pe.matmul(ps_s[:, j % 2, 1, 0:P], q_one[:, s, head, bass.ts(i, P)],
                                             k_two[:, s, c0 * P + HALF:c0 * P + n * P], start=True, stop=True)
                        done.then_inc(scored, 1)

                    def transposes(j):
                        s, i, head, c0, n, col = body[j]
                        pe.wait_ge(exped, base + j + 1)
                        for part, chunks in enumerate((range(3), range(3, n))):
                            pe.wait_ge(turned_sb, 2 * (base + j) + part + 1)
                            for c in chunks:
                                done = pe.transpose(ps_t[:, part, c - chunks[0], :], prob[:, j % 2, bass.ts(c, P)],
                                                    ident[:])
                            done.then_inc(turned, 1)

                    def outputs(j):
                        s, i, head, c0, n, col = body[j]
                        pe.wait_ge(turned_sb, 2 * (base + j) + 4)
                        pe.wait_ge(placed, base + j + 1)
                        for c in range(n):
                            done = pe.matmul(ps_o[:, j % 2, 0, :], probT[:, j % 2, c, :], v_two[:, s, c0 + c, :],
                                             start=(c == 0), stop=(c == n - 1))
                        done.then_inc(summed, 1)

                    scores(0)
                    scores(1)
                    for j in range(ALL):
                        transposes(j)
                        if j + 2 < ALL:
                            scores(j + 2)
                        if j >= 1:
                            outputs(j - 1)
                    outputs(ALL - 1)

            @block.vector
            def _(dve):
                dve.sem_inc(biased, 2)
                dve.sem_inc(placed, 2)
                with dve.Fori(0, PAIRS) as hp:
                    base = hp * ALL

                    def add_bias(j):
                        s, i, head, c0, n, col = body[j]
                        if j % JOBS == 0:
                            dve.wait_ge(loaded[s], 16 * N_LOAD * (hp + 1))
                            dve.wait_ge(stored[s], 16 * (hp + 1))
                        dve.wait_ge(scored, base + j + 1)
                        dve.wait_ge(turned, 2 * (base + j) + 2)
                        dve.sem_inc(stepped, 1)
                        dve.tensor_tensor_reduce(
                            minus_s[:, j % 2, 0:n * P],
                            ps_s[:, j % 2].rearrange("p a n -> p (a n)")[:, 0:n * P],
                            bias[:, s, head, col:col + n * P], -1.0, BIG, ALU.add, ALU.min,
                            rows[:, s, i, 2 * HD + 2 * head:2 * HD + 2 * head + 1]).then_inc(biased, 1)

                    def place(j):
                        s, i, head, c0, n, col = body[j]
                        dve.wait_ge(summed, base + j + 1 + 2 * JOBS)
                        own = slice(HD * head, HD * head + HD)
                        dve.tensor_copy(rows[:, s, i, own], ps_o[:, j % 2, 0, own]).then_inc(placed, 1)

                    for j in range(ALL):
                        add_bias(j)
                        if j >= 3:
                            place(j - 3)
                    for j in range(ALL - 3, ALL):
                        place(j)

            @block.scalar
            def _(act):
                act.sem_inc(turned_sb, 2)
                for s in range(N_SEQ):
                    act.sem_inc(stored[s], 16)
                with act.Fori(0, PAIRS) as hp:
                    base = hp * ALL

                    def store(s):
                        act.wait_ge(placed, (2 * hp + s + 1) * JOBS + 2)
                        act.dma_start(scratch.o[0, bass.ts(s, SEQ), bass.ds(hp * OROW, OROW)].rearrange(
                            "(t p) n -> p t n", p=P), rows[:, s]).then_inc(stored[s], 16)

                    def exps(j):
                        s, i, head, c0, n, col = body[j]
                        act.wait_ge(biased, base + j + 3)
                        act.wait_ge(turned, 2 * (base + j) + 2)
                        at = 2 * HD + 2 * head
                        act.activation(prob[:, j % 2, 0:n * P], minus_s[:, j % 2, 0:n * P], ACT.Exp,
                                       bias=rows[:, s, i, at:at + 1], scale=-1.0,
                                       accum_out=rows[:, s, i, at + 1:at + 2]).then_inc(exped, 1)

                    def copy(j):
                        s, i, head, c0, n, col = body[j]
                        act.wait_ge(summed, base + j - 1 + 2 * JOBS)
                        for part, chunks in enumerate((range(3), range(3, n))):
                            act.wait_ge(turned, 2 * (base + j) + part + 5)
                            act.activation(probT[:, j % 2, chunks[0]:chunks[-1] + 1, :],
                                           ps_t[:, part, 0:len(chunks), :], ACT.Copy).then_inc(turned_sb, 1)

                    for j in range(ALL):
                        exps(j)
                        if j >= 1:
                            copy(j - 1)
                        if j == JOBS + 5:
                            store(0)
                    copy(ALL - 1)
                    store(1)
                for s in range(N_SEQ):
                    act.wait_ge(stored[s], 16 * (PAIRS + 1))


def load_constants(nc, ident, c_ident):
    loaded = nc.alloc_semaphore("ident_loaded")
    with nc.Block() as block:
        @block.sync
        def _(sp):
            sp.dma_start(ident[:], c_ident).then_inc(loaded, 16)
            sp.wait_ge(loaded, 16)


def build(nc, a, y):
    scratch = Scratch(nc)
    with nc.sbuf_tensor("ident", [P, P], F32) as ident:
        load_constants(nc, ident, a["c_ident"])

        def finish_layer(tag, layer, n_g, x, w_o, out):
            with ExitStack() as ctx:
                routing = Routing(ctx, nc, tag)
                merge_and_norm(nc, f"{tag}_mn", n_g, x, w_o, a["ln_g"][layer, 0], a["ln_b"][layer, 0],
                               a["w_rg"][layer], a["b_rg"][layer], a["w_re"][layer], a["b_re"][layer],
                               ident, routing.logits, scratch)
                route_tokens(nc, f"{tag}_rt", routing, a["c_iota"], a["c_before"], scratch)
                experts(nc, f"{tag}_ex", routing, a["w1"][layer], a["w3"][layer], a["w2"][layer], ident, scratch)
                sum_and_norm(nc, f"{tag}_sn", routing, a["ln_g"][layer, 1], a["ln_b"][layer, 1], out, scratch)

        bias_rows(nc, a["t5_table"], a["c_bucket"], scratch)
        project_qkv(nc, "qa", a["x"], a["w_qkv_a"][0], ident, N_DIL, scratch.qT, scratch.kT, scratch.v,
                    clear=(scratch.xs, scratch.ys))
        dilated_attention(nc, ident, scratch)
        finish_layer("a", 0, N_DIL, a["x"], a["w_o_a"][0], scratch.x2)
        grid_bias(nc, a["rpb_b"][0], a["c_edge"], a["c_inner"], scratch)
        project_qkv(nc, "qb", scratch.x2, a["w_qkv_b"][0], ident, 1, scratch.qT, scratch.kT, scratch.v)
        grid_attention(nc, ident, scratch)
        finish_layer("b", 1, 1, scratch.x2, a["w_o_b"][0], y)


def kernel(x_prompt, x_sample, t5_table, w_qkv_a, w_o_a, w_qkv_b, w_o_b, rpb_b, ln_g, ln_b,
           w_rg, b_rg, w_re, b_re, w1, w3, w2):
    import concourse.bacc as bacc
    from concourse.bass_utils import run_bass_kernel_spmd

    arrays = dict(
        x=np.concatenate([np.asarray(x_prompt)[0], np.asarray(x_sample)[0]]),
        t5_table=t5_table, w_qkv_a=w_qkv_a, w_o_a=w_o_a, w_qkv_b=w_qkv_b, w_o_b=w_o_b, rpb_b=rpb_b, ln_g=ln_g,
        ln_b=ln_b, w_rg=w_rg, b_rg=b_rg, w_re=w_re, b_re=b_re, w1=w1, w3=w3, w2=w2, **small_constants())
    arrays = {name: np.ascontiguousarray(value) for name, value in arrays.items()}
    nc = bacc.Bacc("TRN2", target_bir_lowering=False, num_devices=1)
    a = {name: nc.dram_tensor(name, value.shape, F32, kind="ExternalInput").ap() for name, value in arrays.items()}
    y = nc.dram_tensor("y", [TOKENS, D], F32, kind="ExternalOutput")
    build(nc, a, y.ap())
    result = run_bass_kernel_spmd(nc, [arrays], core_ids=[0])
    y = result.results[0]["y"]
    return y[None, :SEQ], y[None, SEQ:]
```
